# Optimizing a Trainium2 kernel written in Bass

```python
import jax, jax.numpy as jnp
from jax import lax
import numpy as np

D_MODEL = 1024
BATCH = 1
SEQ = 512
DEPTH = 1

EPS = 1e-6
N_MEM = 256
BRANCH_WIDTH = 512
N_BRANCH = 3
HG_HEADS = 4
HG_DK = 128
HG_DV = 128
HG_WIDTH = HG_HEADS * HG_DV
HG_CHUNK = 64
SC_WIDTH = BRANCH_WIDTH
SC_KERNEL = 3
MX_HEADS = 4
MX_HD = 128
MX_WIDTH = MX_HEADS * MX_HD
IN_SPLITS = tuple(BRANCH_WIDTH * i for i in range(1, 10))
IN_COLS = 9 * BRANCH_WIDTH + N_BRANCH * D_MODEL
PEER_HEADS = 8
PEER_NKEYS = 128
PEER_N = PEER_NKEYS * PEER_NKEYS
PEER_DQ = 256
PEER_TOPK = 16
PEER_TOKEN_BLOCK = 128

kernel_name = "hybrid_hgrn2_shortconv_memattn_peer_encoder"

def rms_norm(x, g):
    xf = x.astype(jnp.float32)
    y = xf * lax.rsqrt(jnp.mean(xf * xf, axis=-1, keepdims=True) + EPS)
    return (y * g.astype(jnp.float32)).astype(x.dtype)

def hgrn2_chunk_scan(q, k, v, log_f):
    B, S, H, _ = q.shape
    C = HG_CHUNK
    n = S // C
    to_chunks = lambda t: t.reshape(B, n, C, H, t.shape[-1]).transpose(0, 3, 1, 2, 4)
    q, k, v, log_f = map(to_chunks, (q, k, v, log_f))
    G = jnp.cumsum(log_f, axis=3)
    G_ref = G[:, :, :, C // 2 - 1:C // 2, :]
    q_r = q * jnp.exp(G - G_ref)
    k_r = k * jnp.exp(G_ref - G)
    scores = jnp.einsum('bhncd,bhnsd->bhncs', q_r, k_r)
    mask = jnp.tril(jnp.ones((C, C), dtype=bool))
    intra = jnp.einsum('bhncs,bhnse->bhnce', jnp.where(mask, scores, 0.0), v)
    G_last = G[:, :, :, -1:, :]
    dS = jnp.einsum('bhncd,bhnce->bhnde', k * jnp.exp(G_last - G), v)
    decay = jnp.exp(G_last[:, :, :, 0, :])

    def step(S_prev, inp):
        dS_c, dec_c = inp
        return dec_c[..., None] * S_prev + dS_c, S_prev

    S0 = jnp.zeros((B, H, q.shape[-1], v.shape[-1]), jnp.float32)
    _, S_start = lax.scan(step, S0, (jnp.moveaxis(dS, 2, 0), jnp.moveaxis(decay, 2, 0)))
    S_start = jnp.moveaxis(S_start, 0, 2)
    inter = jnp.einsum('bhncd,bhnde->bhnce', q * jnp.exp(G), S_start)
    o = intra + inter
    return o.transpose(0, 2, 3, 1, 4).reshape(B, S, H, v.shape[-1])

def hgrn2_direction(q, v, z, lb, reverse):
    B, S = z.shape[:2]
    zf = z.astype(jnp.float32)
    log_f = jnp.log(lb + (1.0 - lb) * jax.nn.sigmoid(zf))
    k = (1.0 - lb) * jax.nn.sigmoid(-zf)
    heads = lambda t: t.reshape(B, S, HG_HEADS, HG_DK)
    args = (heads(q), heads(k), v.reshape(B, S, HG_HEADS, HG_DV), heads(log_f))
    if reverse:
        args = tuple(jnp.flip(t, axis=1) for t in args)
    o = hgrn2_chunk_scan(*args)
    return jnp.flip(o, axis=1) if reverse else o

def token_mixers(h, mem, w_in, lb, hg_norm_g, sc_conv_w, mem_norm_g, w_mem_kv, w_branch, w_out):
    B, S, _ = h.shape
    proj = h @ w_in
    hq, hi, hf_fwd, hf_bwd, hg, sb, sc, sh, mq, gates = jnp.split(proj, IN_SPLITS, axis=-1)

    q = jax.nn.silu(hq.astype(jnp.float32))
    v = hi.astype(jnp.float32)
    o = hgrn2_direction(q, v, hf_fwd, lb[0], False) + hgrn2_direction(q, v, hf_bwd, lb[1], True)
    o = o * lax.rsqrt(jnp.mean(o * o, axis=-1, keepdims=True) + EPS)
    y_hg = (o.reshape(B, S, HG_WIDTH) * hg_norm_g.astype(jnp.float32)
            * jax.nn.silu(hg.astype(jnp.float32))).astype(h.dtype)

    u = sc * sh
    conv = lax.conv_general_dilated(u, sc_conv_w[:, None, :], window_strides=(1,), padding='SAME',
                                    dimension_numbers=('NWC', 'WIO', 'NWC'),
                                    feature_group_count=SC_WIDTH)
    y_sc = sb * conv

    m = rms_norm(mem, mem_norm_g)
    mk, mv = jnp.split(m @ w_mem_kv, 2, axis=-1)
    qh = mq.reshape(B, S, MX_HEADS, MX_HD)
    kh = mk.reshape(B, N_MEM, MX_HEADS, MX_HD)
    vh = mv.reshape(B, N_MEM, MX_HEADS, MX_HD)
    logits = jnp.einsum('bshd,bmhd->bhsm', qh, kh).astype(jnp.float32) * (MX_HD ** -0.5)
    p = jax.nn.softmax(logits, axis=-1).astype(h.dtype)
    y_mx = jnp.einsum('bhsm,bmhd->bshd', p, vh).reshape(B, S, MX_WIDTH)

    branches = jnp.stack([y_hg, y_sc, y_mx], axis=2)
    projected = jnp.einsum('bsnc,ncd->bsnd', branches, w_branch)
    gate = jax.nn.sigmoid(gates.reshape(B, S, N_BRANCH, D_MODEL))
    merged = jnp.sum(gate * projected, axis=2)
    return merged @ w_out

def peer(h, w_q, sub_keys, u, v):
    B, S, D = h.shape
    T = B * S
    hf = h.reshape(T, D)
    q = (hf @ w_q).reshape(T, PEER_HEADS, 2, PEER_DQ // 2).astype(jnp.float32)
    s = jnp.einsum('thpd,hpkd->thpk', q, sub_keys.astype(jnp.float32))
    top_s, top_i = lax.top_k(s, PEER_TOPK)
    cand_s = (top_s[:, :, 0, :, None] + top_s[:, :, 1, None, :]).reshape(T, PEER_HEADS, -1)
    cand_i = (top_i[:, :, 0, :, None] * PEER_NKEYS + top_i[:, :, 1, None, :]).reshape(T, PEER_HEADS, -1)
    best_s, best_pos = lax.top_k(cand_s, PEER_TOPK)
    expert_idx = jnp.take_along_axis(cand_i, best_pos, axis=-1)
    gate = jax.nn.softmax(best_s, axis=-1).astype(h.dtype)

    nb = T // PEER_TOKEN_BLOCK

    def block(args):
        xb, idxb, gb = args
        ub = jnp.take(u, idxb, axis=0)
        act = jax.nn.gelu(jnp.einsum('td,thkd->thk', xb, ub), approximate=False)
        vb = jnp.take(v, idxb, axis=0)
        return jnp.einsum('thk,thkd->td', gb * act, vb)

    out = lax.map(block, (hf.reshape(nb, PEER_TOKEN_BLOCK, D),
                          expert_idx.reshape(nb, PEER_TOKEN_BLOCK, PEER_HEADS, PEER_TOPK),
                          gate.reshape(nb, PEER_TOKEN_BLOCK, PEER_HEADS, PEER_TOPK)))
    return out.reshape(B, S, D)

def setup_inputs(seed: int = 0) -> dict:
    key = jax.random.key(seed)
    ks = jax.random.split(key, 20)
    f32 = jnp.float32
    nrm = lambda k, shape, scale: jax.random.normal(k, shape, f32) * scale
    gain = lambda k, shape: 1.0 + 0.05 * jax.random.normal(k, shape, f32)
    return {
        "x": nrm(ks[0], (BATCH, SEQ, D_MODEL), 1.0),
        "mem": nrm(ks[1], (BATCH, N_MEM, D_MODEL), 1.0),
        "norm_mix_g": gain(ks[2], (DEPTH, D_MODEL)),
        "w_in": nrm(ks[3], (DEPTH, D_MODEL, IN_COLS), D_MODEL ** -0.5),
        "hg_lb": nrm(ks[4], (DEPTH + 1, 2, HG_WIDTH), 0.1),
        "hg_norm_g": gain(ks[5], (DEPTH, HG_WIDTH)),
        "sc_conv_w": nrm(ks[6], (DEPTH, SC_KERNEL, SC_WIDTH), SC_KERNEL ** -0.5),
        "mem_norm_g": gain(ks[7], (DEPTH, D_MODEL)),
        "w_mem_kv": nrm(ks[8], (DEPTH, D_MODEL, 2 * MX_WIDTH), D_MODEL ** -0.5),
        "w_branch": nrm(ks[9], (DEPTH, N_BRANCH, BRANCH_WIDTH, D_MODEL), BRANCH_WIDTH ** -0.5),
        "w_out": nrm(ks[10], (DEPTH, D_MODEL, D_MODEL), D_MODEL ** -0.5),
        "norm_ffn_g": gain(ks[11], (DEPTH, D_MODEL)),
        "peer_w_q": nrm(ks[12], (DEPTH, D_MODEL, PEER_HEADS * PEER_DQ), D_MODEL ** -0.5),
        "peer_sub_keys": nrm(ks[13], (DEPTH, PEER_HEADS, 2, PEER_NKEYS, PEER_DQ // 2), (PEER_DQ // 2) ** -0.5),
        "peer_u": nrm(ks[14], (DEPTH, PEER_N, D_MODEL), D_MODEL ** -0.5),
        "peer_v": nrm(ks[15], (DEPTH, PEER_N, D_MODEL), D_MODEL ** -0.5),
        "final_norm_g": gain(ks[16], (D_MODEL,)),
    }

def reference(x, mem, norm_mix_g, w_in, hg_lb, hg_norm_g, sc_conv_w, mem_norm_g, w_mem_kv,
              w_branch, w_out, norm_ffn_g, peer_w_q, peer_sub_keys, peer_u, peer_v, final_norm_g):
    lb_table = jnp.cumsum(jax.nn.softmax(hg_lb.astype(jnp.float32), axis=0), axis=0)
    for l in range(DEPTH):
        h = rms_norm(x, norm_mix_g[l])
        x = x + token_mixers(h, mem, w_in[l], lb_table[l], hg_norm_g[l], sc_conv_w[l],
                             mem_norm_g[l], w_mem_kv[l], w_branch[l], w_out[l])
        h = rms_norm(x, norm_ffn_g[l])
        x = x + peer(h, peer_w_q[l], peer_sub_keys[l], peer_u[l], peer_v[l])
    return rms_norm(x, final_norm_g)


_drawn_inputs = setup_inputs


def setup_inputs(seed=0):
    import zlib

    import numpy as np

    out = dict(_drawn_inputs(seed))
    spreads = {}
    factors = {'hg_lb': 8.0,
     'hg_norm_g': 4.009,
     'mem_norm_g': 8.0,
     'norm_ffn_g': 8.0,
     'peer_w_q': 4.457,
     'peer_sub_keys': 4.439,
     'peer_u': 4.87,
     'peer_v': 4.419}
    for name, (base, spread) in spreads.items():
        noise = np.random.default_rng([zlib.crc32(name.encode()), seed]).standard_normal(out[name].shape)
        drawn = base * np.exp(spread * noise) if base else spread * noise
        out[name] = __import__('jax').numpy.asarray(drawn.astype(out[name].dtype))
    for name, factor in factors.items():
        out[name] = (out[name] * factor).astype(out[name].dtype)
    return out
```

```python
from contextlib import ExitStack

import numpy as np

import concourse.bass as bass
from concourse import mybir

F32 = mybir.dt.float32
U32 = mybir.dt.uint32
BF16 = mybir.dt.bfloat16
ALU = mybir.AluOpType
ACT = mybir.ActivationFunctionType
AX_X = mybir.AxisListType.X

P = 128
T = 512
D = 1024
KD = D // P
NT = T // P
HALF = 256
TPH = HALF // P
HALVES = T // HALF
NMEM = 256
H = 4
CH = 64
NCH = T // CH
BW = 512
BC = BW // P
EPS = 1e-6
NEG = -3.0e38
HP = 16
PH = 8
NK = 128
TOP = 16
SLOTS = PH * TOP
RING = 6
GROUP = 2
WSLOTS = 4
WCOLS = 256
CAND_ROWS = ((0, 1, 16), (1, 1, 8), (2, 1, 5), (3, 1, 4), (4, 4, 3), (8, 8, 1))
NCAND = sum(ni * nj for _, ni, nj in CAND_ROWS)
COL_Q, COL_V, COL_F, COL_B, COL_HG, COL_SB, COL_SC, COL_SH, COL_MQ, COL_GATE = (BW * i for i in range(10))
C_ID, C_ONE, C_ZERO, C_IOTA = 0, 128, 256, 384
C_N = C_IOTA + NCAND
S_MF, S_MB, S_KEEP = 0, 128, 256
S_N = S_KEEP + T
V_MIX, V_MEM, V_LB, V_HG, V_CONV = 0, 8, 16, 32, 36
V_N = 48
BRANCH_ORDER = (1, 2, 0)


def constants():
    c, m = np.zeros((P, C_N), np.float32), np.zeros((P, S_N), np.float32)
    c[:, C_ID:C_ID + P] = np.eye(P)
    c[:, C_ONE:C_ONE + P] = 1.0
    s, t = np.arange(P)[:, None], np.arange(P)[None, :]
    same = s // CH == t // CH
    m[:, S_MF:S_MF + P] = same & (s <= t)
    m[:, S_MB:S_MB + P] = same & (s >= t)
    m[:, S_KEEP:S_KEEP + T] = np.arange(T) % CH != 0
    c[:, C_IOTA:] = np.arange(NCAND)
    return c, m


def plan():
    steps = [("norm_in",), ("norm_mem",)]
    steps += [("kv", b) for b in range(4)]
    steps += [("z", d, b) for d in range(2) for b in range(2)]
    steps += [("q", b) for b in range(2)] + [("v", b) for b in range(2)]

    def mixers(f):
        conv = [("conv", f, b) for b in range(2)]
        mq = [("mq", f, b) for b in range(2)]
        att = [("att", f, h) for h in range(H)]
        br = {n: [("branch", f, n, b) for b in range(4)] for n in range(3)}
        return conv, mq, att, br

    def peer_in(f):
        s = [("wout", f, b) for b in range(4)]
        s += [("ffn", f), ("turn", f)]
        s += [("pq", f, b) for b in range(HP // 2)]
        return s

    def topk(t):
        return [("top1", t, g) for g in range(4)] + [("top2", t)] + [("top3", t, g) for g in range(2)] + \
            [("look", t, g) for g in range(2)] + [("gate", t)]

    conv, mq, att, br = mixers(0)
    side = conv + mq + br[1]
    elem = [("logf",)]
    for h in range(H):
        elem += [("elem", h, 0), ("elem", h, 1), "side", ("intra", h, 0), "side", ("intra", h, 1), ("o", h)]
    for s in elem:
        if s == "side":
            steps.append(side.pop(0)) if side else None
        else:
            steps.append(s)
    steps += side + att + br[2] + [("hg", 0, b) for b in range(2)] + br[0] + peer_in(0)
    steps += topk(0)

    conv, mq, att, br = mixers(1)
    rest = topk(1) + conv + mq + br[1] + att + br[2] + [("hg", 1, b) for b in range(2)] + br[0] + peer_in(1) + topk(2) + topk(3)
    for t in range(NT):
        steps.append(("open", t))
        k = 0
        while k < SLOTS:
            n = min(RING, SLOTS - k)
            if not rest:
                n = SLOTS - k
            steps.append(("gather", t, k, n))
            k += n
            if rest and k < SLOTS:
                steps += rest[:3]
                rest = rest[3:]
        steps.append(("drain", t))
        if t == NT - 1:
            assert not rest
        steps.append(("last", t))
    return steps


def chunks_of(step):
    k = step[0]
    if k in ("norm_in", "norm_mem"):
        return [("A", step)]
    if k == "kv":
        return [("A", (*step, c)) for c in range(2)]
    if k in ("z", "q"):
        return [("A", (*step, c)) for c in range(2)]
    if k == "v":
        return [("A", (*step, t)) for t in range(NT)]
    if k == "conv":
        return [(r, (*step, w, c)) for r, w in (("A", "C"), ("B", "h"), ("B", "B")) for c in range(2)]
    if k == "mq":
        return [("A", (*step, c)) for c in range(2)]
    if k == "branch":
        return [(r, (*step, w, c)) for c in range(2) for r, w in (("A", "gate"), ("B", "br"))]
    if k == "hg":
        return [("A", (*step, w, c)) for c in range(2) for w in ("z", "ss")]
    if k == "wout":
        return [("B", (*step, t)) for t in range(TPH)]
    if k == "turn":
        return [("A", (*step, t, g)) for t in range(TPH) for g in range(2)]
    if k == "pq":
        return [("A", (*step, "q", 0)), ("A", (*step, "q", 1)), ("A", (*step, "s", 0)), ("A", (*step, "s", 1))]
    return []


def weights_of(step):
    k = step[0]
    if k == "kv":
        return [("kv", 0, D, WCOLS * step[1], WCOLS)]
    if k == "z":
        return [("in", 0, D, (COL_F, COL_B)[step[1]] + WCOLS * step[2], WCOLS)]
    if k == "q":
        return [("in", 0, D, COL_Q + WCOLS * step[1], WCOLS)]
    if k == "v":
        return [("in", 0, D, COL_V + WCOLS * step[1], WCOLS)]
    if k == "conv":
        return [("in", 0, D, c + WCOLS * step[2], WCOLS) for c in (COL_SC, COL_SH, COL_SB)]
    if k == "mq":
        return [("in", 0, D, COL_MQ + WCOLS * step[2], WCOLS)]
    if k == "hg":
        return [("in", 0, D, COL_HG + WCOLS * step[2], WCOLS)]
    if k == "branch":
        _, _, n, b = step
        return [("in", 0, D, COL_GATE + D * n + WCOLS * b, WCOLS), ("br", BW * n, BW, WCOLS * b, WCOLS)]
    if k == "wout":
        return [("out", 0, D, WCOLS * step[2], WCOLS)]
    if k == "pq":
        return [("pq", 0, D, WCOLS * step[2], WCOLS)]
    return []


def build(nc, a, out):
    steps = plan()
    order = {"A": [], "B": []}
    last_piece = {}
    blocks, block_of = [], {}
    for s in steps:
        for r, key in chunks_of(s):
            order[r].append(key)
            last_piece[s] = (r, key)
        for i, w in enumerate(weights_of(s)):
            block_of[s, i] = len(blocks)
            blocks.append((s, w))
    place = {r: {key: i for i, key in enumerate(o)} for r, o in order.items()}

    with ExitStack() as ctx:
        def sb(name, shape, dt=F32):
            return ctx.enter_context(nc.sbuf_tensor(name, shape, dt))

        def sem(name):
            return ctx.enter_context(nc.semaphore(name))

        cst = sb("cst", [P, C_N])
        ident, ones, zeros = cst[:, C_ID:C_ID + P], cst[:, C_ONE:C_ONE + P], cst[:, C_ZERO:C_ZERO + P]
        vec = sb("vec", [P, V_N])
        lbs = sb("lbs", [P, 3, 8])
        eps = sb("eps", [P, 1])
        keys = sb("keys", [P, HP * NK])
        g_ffn = sb("g_ffn", [P, D])
        g_fin = sb("g_fin", [P, D])
        hT = sb("hT", [P, KD, T])
        W = sb("W", [P, WSLOTS, KD * WCOLS])
        mkT = sb("mkT", [P, H, NMEM])
        mv = sb("mv", [P, NMEM // P, BW])
        oT = sb("oT", [P, H, T])
        ys = sb("ys", [P, 4096])
        y = [ys[:, n * BC * HALF:(n + 1) * BC * HALF].rearrange("p (c t) -> p c t", c=BC) for n in range(3)]
        score = ys[:, :].rearrange("p (t k) -> p t k", t=TPH)
        mx = sb("mx", [P, KD * HALF])
        merged = mx[:, :].rearrange("p (k t) -> p k t", k=KD)
        mqT = y[2]
        prob = ys[:, 3 * BC * HALF:3 * BC * HALF + 512].rearrange("p (t m) -> p t m", t=TPH)
        probT = ys[:, 3 * BC * HALF + 512:4096].rearrange("p (m t) -> p m t", m=2)
        WIN = HALF + 1
        csb = sb("csb", [P, 2, WIN])
        ub = sb("ub", [P, 2, HALF + 2])
        gsb = sb("gsb", [P, 2, HALF])
        tmp = sb("tmp", [P, 2, HALF])
        qpT = sb("qpT", [P, 2, HALF])
        tiny = sb("tiny", [P, 32])
        acts = sb("acts", [P, 3, RING])
        stage = sb("stage", [P, RING, 1], U32)
        diag = sb("diag", [P, RING, P])
        junk = qpT[:, :, :].rearrange("p c t -> p (c t)").bitcast(BF16)
        AR = RING * 2 * D + NT * D + TPH * D + 3 * HP * TOP + 2 * PH * NCAND + 3 * SLOTS + TOP * NCAND + 2 * NT * SLOTS
        arena = sb("arena", [P, AR])
        at = [0]

        def cut(n):
            at[0] += n
            assert at[0] <= AR, at[0]
            return arena[:, at[0] - n:at[0]]

        sig = cut(2 * H * T).rearrange("p (d h t) -> p d h t", d=2, h=H)
        sgn = cut(2 * H * T).rearrange("p (d h t) -> p d h t", d=2, h=H)
        sqx = arena[:, 0:KD * T].rearrange("p (k t) -> p k t", k=KD)
        memT = arena[:, KD * T:KD * T + KD * NMEM].rearrange("p (k t) -> p k t", k=KD)
        sqm = arena[:, KD * T + KD * NMEM:KD * T + 2 * KD * NMEM].rearrange("p (k t) -> p k t", k=KD)
        qT = cut(H * T).rearrange("p (h t) -> p h t", h=H)
        v = cut(NT * BW).rearrange("p (t e) -> p t e", t=NT)
        cumG, dref, expn, dlast = ([cut(T) for _ in range(2)] for _ in range(4))
        kdn = [cut(NT * 2 * P).rearrange("p (j i d) -> p j i d", j=NT, i=2) for _ in range(2)]
        PT = [cut(NT * P) for _ in range(2)]
        state = [cut(NCH * P).rearrange("p (n e) -> p n e", n=NCH) for _ in range(2)]
        decay = [cut(NCH) for _ in range(2)]
        hcst = cut(S_N)
        at[0] = 0
        ring = cut(RING * 2 * D).rearrange("p (s n) -> p s n", s=RING)
        h2 = cut(NT * D).rearrange("p (t n) -> p t n", t=NT)
        x2 = cut(TPH * D).rearrange("p (t n) -> p t n", t=TPH)
        tv, tif = (cut(HP * TOP).rearrange("p (s k) -> p s k", s=HP) for _ in range(2))
        ti = cut(HP * TOP).bitcast(U32).rearrange("p (s k) -> p s k", s=HP)
        cs, ci = (cut(PH * NCAND).rearrange("p (h c) -> p h c", h=PH) for _ in range(2))
        bs, posf = (cut(SLOTS).rearrange("p (h k) -> p h k", h=PH) for _ in range(2))
        pos = cut(SLOTS).bitcast(U32).rearrange("p (h k) -> p h k", h=PH)
        eq = cut(TOP * NCAND).rearrange("p (k c) -> p k c", k=TOP)
        gate = cut(NT * SLOTS).rearrange("p (t s) -> p t s", t=NT)
        idx = cut(NT * SLOTS).bitcast(U32).rearrange("p (t s) -> p t s", t=NT)
        x2_dram = nc.dram_tensor("x2_kept", (T, D), F32, kind="Internal").ap()

        banks = [ctx.enter_context(nc.psum_tensor(f"bank{i}", [P, 512], F32)) for i in range(6)]
        wide = ctx.enter_context(nc.psum_tensor("wide", [P, 1024], F32))
        bankA, bankB = banks[0:2], banks[2:4]
        tp, scb = banks[4], banks[5]

        x_in, c_in, mem_in, late_in = sem("x_in"), sem("c_in"), sem("mem_in"), sem("late_in")
        w_in = [sem(f"w_in{i}") for i in range(WSLOTS)]
        A_full, A_free = sem("A_full"), sem("A_free")
        B_full, B_free = sem("B_full"), sem("B_free")
        v_ord, a_ord = sem("v_ord"), sem("a_ord")
        sq_done, root, eps_done, lb_exp = sem("sq_done"), sem("root"), sem("eps_done"), sem("lb_exp")
        h_done, m_done = sem("h_done"), sem("m_done")
        lb_done = sem("lb_done")
        zero_done = sem("zero_done")
        logf_done = sem("logf_done")
        dsub, exps, prods = sem("dsub"), sem("exps"), sem("prods")
        kd_turned, kd_copied = sem("kd_turned"), sem("kd_copied")
        sc_made, sc_masked = sem("sc_made"), sem("sc_masked")
        ds_made, st_done = sem("ds_made"), sem("st_done")
        o_made, o_kept = sem("o_made"), sem("o_kept")
        y1_done = sem("y1_done")
        lg_made, mx_done, pexp, pnorm = sem("lg_made"), sem("mx_done"), sem("pexp"), sem("pnorm")
        p_turned, pT_done, pv_made, y2_done = sem("p_turned"), sem("pT_done"), sem("pv_made"), sem("y2_done")
        osq_done, y0_done = sem("osq_done"), sem("y0_done")
        x_nat, x2_kept = sem("x_nat"), sem("x2_kept")
        ssq_done, h2_done = sem("ssq_done"), sem("h2_done")
        gd_done, ge_done, idx_done, gate_done = sem("gd_done"), sem("ge_done"), sem("idx_done"), sem("gate_done")
        landed = [sem(f"landed{i}") for i in range(RING)]
        staged, seen = sem("staged"), sem("seen")
        dot, gel, wgt, dia, used = sem("dot"), sem("gel"), sem("wgt"), sem("dia"), sem("used")
        back_in, drained, fsq, fdone, out_done = sem("back_in"), sem("drained"), sem("fsq"), sem("fdone"), sem("out_done")
        top1_done, lb_diff = sem("top1_done"), sem("lb_diff")
        last_before_hg = {}
        for f in range(HALVES):
            before = steps[:steps.index(("hg", f, 0))]
            last_before_hg[f] = [key for s in before for r, key in chunks_of(s) if r == "B"][-1]

        full = {"A": A_full, "B": B_full}
        free = {"A": A_free, "B": B_free}

        def n_of(r, key):
            return place[r][key] + 1

        def bank_of(r, key):
            return (bankA if r == "A" else bankB)[place[r][key] % 2]

        def wblock(step, i):
            b = block_of[step, i]
            kc = blocks[b][1][2] // P
            return W[:, b % WSLOTS, 0:kc * WCOLS].rearrange("p (k n) -> p k n", k=kc)

        def window(f):
            return (0, 0 + HALF + 1, 1) if f == 0 else (HALF - 1, HALF + 1, 0)

        src = {"in": a["w_in"], "kv": a["w_kv"], "br": a["w_br"], "out": a["w_out"], "pq": a["w_pq"]}
        xn = a["x"].rearrange("(t p) n -> t p n", p=P)
        outn = out.rearrange("b (t p) n -> (b t) p n", p=P)
        x2n = x2_dram.rearrange("(t p) n -> t p n", p=P)

        def land_count(g):
            return 16 * (g // RING + 1)

        block = ctx.enter_context(nc.Block())

        @block.sync
        def _(sp):
            xT_v = a["xT"].rearrange("(k p) t -> p k t", p=P)
            for i in range(4):
                sp.dma_start(hT[:, 2 * i:2 * i + 2, :], xT_v[:, 2 * i:2 * i + 2, :]).then_inc(x_in, 16)
            sp.dma_start(cst[:, :], a["cst"]).then_inc(c_in, 16)
            sp.dma_start(vec[:, :], a["vec"]).then_inc(c_in, 16)
            sp.dma_start(hcst, a["hcst"]).then_inc(c_in, 16)
            sp.dma_start(memT, a["memT"].rearrange("(k p) t -> p k t", p=P)).then_inc(mem_in, 16)
            spill_at = {b: s[1] for b, (s, _) in enumerate(blocks) if s[0] == "pq" and s[2] == 5}
            xload_at = {b: s[1] for b, (s, _) in enumerate(blocks) if s[0] == "wout" and s[2] == 0}
            for b, (s, (name, r0, rows, c0, cols)) in enumerate(blocks):
                if b >= WSLOTS:
                    r, key = last_piece[blocks[b - WSLOTS][0]]
                    sp.wait_ge(full[r], n_of(r, key))
                kc = rows // P
                sp.dma_start(W[:, b % WSLOTS, 0:kc * cols].rearrange("p (k n) -> p k n", k=kc),
                             src[name][r0:r0 + rows, c0:c0 + cols].rearrange("(k p) n -> p k n", p=P))\
                  .then_inc(w_in[b % WSLOTS], 16)
                if b == 5:
                    sp.dma_start(keys[:, :], a["keys"]).then_inc(late_in, 16)
                    sp.dma_start(g_ffn[:, :], a["g_ffn"]).then_inc(late_in, 16)
                    sp.dma_start(g_fin[:, :], a["g_fin"]).then_inc(late_in, 16)
                if b in xload_at:
                    f = xload_at[b]
                    if f == 0:
                        sp.wait_ge(o_kept, H)
                    else:
                        sp.wait_ge(x2_kept, 16 * TPH * f)
                        sp.wait_ge(h2_done, TPH * f)
                    for t in range(TPH):
                        sp.dma_start(x2[:, t, :], xn[TPH * f + t]).then_inc(x_nat, 16)
                if b in spill_at:
                    f = spill_at[b]
                    sp.wait_ge(B_free, n_of("B", ("wout", f, 3, TPH - 1)))
                    for t in range(TPH):
                        sp.dma_start(x2n[TPH * f + t], x2[:, t, :]).then_inc(x2_kept, 16)
            sp.wait_ge(x2_kept, 16 * NT)
            sp.wait_ge(out_done, 16 * NT)

        @block.gpsimd
        def _(pool):
            def issue(t, k, s, it):
                g = t * SLOTS + k
                pool.wait_ge(used, it * RING + (g + 1))
                col = idx[:, t, bass.ds(it * RING + k, 1)] if not isinstance(it, int) else idx[:, t, k:k + 1]
                nc.gpsimd.tensor_copy(stage[:, s, :], col).then_inc(staged, 1)
                pool.wait_ge(staged, it * RING + (g + 1))
                pool.sem_inc(seen, 1)
                pool.indirect_dma_start(ring[:, s, :], None, a["uv"],
                                        bass.IndirectOffsetOnAxis(ap=stage[:, s, :], axis=0)).then_inc(landed[s], 16)

            for t in range(NT):
                pool.wait_ge(idx_done, t + 1)
                if t == 0:
                    pool.wait_ge(o_kept, H)
                whole = SLOTS // RING
                with pool.Fori(0, whole) as it:
                    for s in range(RING):
                        issue(t, s, (t * SLOTS + s) % RING, it)
                for k in range(whole * RING, SLOTS):
                    issue(t, k, (t * SLOTS + k) % RING, 0)

        @block.tensor
        def _(pe):
            mm = nc.tensor.matmul

            def open_piece(r, key):
                n = n_of(r, key)
                if n > 2:
                    pe.wait_ge(free[r], n - 2)
                return bank_of(r, key)

            def need_weights(step, i):
                b = block_of[step, i]
                pe.wait_ge(w_in[b % WSLOTS], 16 * (b // WSLOTS + 1))
                return wblock(step, i)

            def project(r, key, outp, lhs, rhs, kc=KD):
                for k in range(kc):
                    last = mm(outp, lhs(k), rhs(k), start=(k == 0), stop=(k == kc - 1))
                last.then_inc(full[r], 1)

            def products(t, k, s, it):
                g = t * SLOTS + k
                pe.wait_ge(dia, it * RING + (g + 1))
                for c in range(2):
                    last = mm(wide[:, 512 * c:512 * c + 512], diag[:, s, :], ring[:, s, D + 512 * c:D + 512 * c + 512],
                              start=False, stop=False, skip_group_check=True)
                last.then_inc(used, 1)

            for step in steps:
                kind = step[0]
                pieces = chunks_of(step)
                if kind in ("norm_in", "norm_mem"):
                    bank = open_piece(*pieces[0])
                    sq, n, c0 = (sqx, T, 0) if kind == "norm_in" else (sqm, NMEM, KD)
                    pe.wait_ge(c_in, 48)
                    for k in range(KD):
                        pe.wait_ge(sq_done, c0 + k + 1)
                        last = mm(bank[:, 0:n], ones, sq[:, k, :], start=(k == 0), stop=(k == KD - 1))
                    last.then_inc(A_full, 1)
                elif kind == "kv":
                    b = step[1]
                    w = need_weights(step, 0)
                    pe.wait_ge(m_done, KD)
                    for c in range(2):
                        r, key = pieces[c]
                        bank = open_piece(r, key)
                        if b < 2:
                            project(r, key, bank[:, 0:NMEM], lambda k: w[:, k, c * P:c * P + P], lambda k: memT[:, k, :])
                        else:
                            project(r, key, bank[:, 0:WCOLS], lambda k: memT[:, k, c * P:c * P + P], lambda k: w[:, k, :])
                elif kind in ("z", "q"):
                    w = need_weights(step, 0)
                    pe.wait_ge(h_done, KD)
                    for c in range(2):
                        r, key = pieces[c]
                        bank = open_piece(r, key)
                        project(r, key, bank[:, :], lambda k: w[:, k, c * P:c * P + P], lambda k: hT[:, k, :])
                elif kind == "v":
                    w = need_weights(step, 0)
                    for t in range(NT):
                        r, key = pieces[t]
                        bank = open_piece(r, key)
                        project(r, key, bank[:, 0:WCOLS], lambda k: hT[:, k, t * P:t * P + P], lambda k: w[:, k, :])
                elif kind == "conv":
                    t0, n, _ = window(step[1])
                    for i in range(3):
                        w = need_weights(step, i)
                        for c in range(2):
                            r, key = pieces[2 * i + c]
                            bank = open_piece(r, key)
                            if i < 2:
                                project(r, key, bank[:, 0:n], lambda k: w[:, k, c * P:c * P + P],
                                        lambda k: hT[:, k, t0:t0 + n])
                            else:
                                project(r, key, bank[:, 0:HALF], lambda k: w[:, k, c * P:c * P + P],
                                        lambda k: hT[:, k, step[1] * HALF:(step[1] + 1) * HALF])
                elif kind == "mq":
                    w = need_weights(step, 0)
                    f = step[1]
                    for c in range(2):
                        r, key = pieces[c]
                        bank = open_piece(r, key)
                        project(r, key, bank[:, 0:HALF], lambda k: w[:, k, c * P:c * P + P],
                                lambda k: hT[:, k, f * HALF:(f + 1) * HALF])
                elif kind == "branch":
                    _, f, n, b = step
                    wg, wb = need_weights(step, 0), need_weights(step, 1)
                    done = {1: (y1_done, BC), 2: (y2_done, H), 0: (y0_done, H)}[n]
                    for c in range(2):
                        r, key = pieces[2 * c]
                        bank = open_piece(r, key)
                        project(r, key, bank[:, 0:HALF], lambda k: wg[:, k, c * P:c * P + P],
                                lambda k: hT[:, k, f * HALF:(f + 1) * HALF])
                        r, key = pieces[2 * c + 1]
                        bank = open_piece(r, key)
                        pe.wait_ge(done[0], done[1] * (f + 1))
                        project(r, key, bank[:, 0:HALF], lambda k: wb[:, k, c * P:c * P + P],
                                lambda k: y[n][:, k, :], BC)
                elif kind == "hg":
                    _, f, b = step
                    w = need_weights(step, 0)
                    for c in range(2):
                        h = 2 * b + c
                        r, key = pieces[2 * c]
                        bank = open_piece(r, key)
                        project(r, key, bank[:, 0:HALF], lambda k: w[:, k, c * P:c * P + P],
                                lambda k: hT[:, k, f * HALF:(f + 1) * HALF])
                        r, key = pieces[2 * c + 1]
                        bank = open_piece(r, key)
                        pe.wait_ge(osq_done, f * H + h + 1)
                        mm(bank[:, 0:HALF], ones, tmp[:, c, :], start=True, stop=True).then_inc(A_full, 1)
                elif kind == "intra":
                    _, h, d = step
                    u = 2 * h + d
                    pe.wait_ge(prods, 4 * u + 4)
                    if u >= 1:
                        pe.wait_ge(kd_copied, u)
                    if d == 0 and h >= 1:
                        pe.wait_ge(o_kept, h)
                    for j in range(NT):
                        last = nc.tensor.transpose(tp[:, j * P:j * P + P], dlast[d][:, j * P:j * P + P], ident)
                    last.then_inc(kd_turned, 1)
                    if u >= 1:
                        pe.wait_ge(sc_masked, u)
                    for j in range(NT):
                        cols = slice(j * P, j * P + P)
                        last = mm(scb[:, cols], expn[d][:, cols], dref[d][:, cols], start=True, stop=True)
                    last.then_inc(sc_made, 1)
                    pe.wait_ge(kd_copied, u + 1)
                    if u >= 1:
                        pe.wait_ge(st_done, u)
                    for n in range(NCH):
                        last = mm(wide[:, n * P:n * P + P], kdn[d][:, n // 2, n % 2, :],
                                  v[:, n // 2, h * P:h * P + P], start=True, stop=True)
                    last.then_inc(ds_made, 1)
                elif kind == "o":
                    h = step[1]
                    pe.wait_ge(sc_masked, 2 * h + 2)
                    pe.wait_ge(st_done, 2 * h + 2)
                    for j in range(NT):
                        cols = slice(j * P, j * P + P)
                        vj = v[:, j, h * P:h * P + P]
                        mm(tp[:, cols], vj, PT[0][:, cols], start=True, stop=False, skip_group_check=True)
                        last = mm(tp[:, cols], vj, PT[1][:, cols], start=False, stop=False, skip_group_check=True)
                        work = [(d, n) for n in (2 * j, 2 * j + 1) for d in range(2)
                                if not (d == 0 and n == 0) and not (d == 1 and n == NCH - 1)]
                        for d, n in work:
                            cc = slice(n * CH, n * CH + CH)
                            last = mm(tp[:, cc], state[d][:, n, :], cumG[d][:, cc], start=False,
                                      stop=(d, n) == work[-1], skip_group_check=True)
                    last.then_inc(o_made, 1)
                elif kind == "att":
                    _, f, h = step
                    u = H * f + h
                    r_mq = ("A", ("mq", f, h // 2, h % 2))
                    pe.wait_ge(A_free, n_of(*r_mq))
                    if u >= 1:
                        pe.wait_ge(pexp, TPH * u)
                    else:
                        pe.wait_ge(sc_masked, 2 * H)
                        pe.wait_ge(o_kept, H)
                    for t in range(TPH):
                        last = mm(scb[:, t * NMEM:(t + 1) * NMEM], mqT[:, h, t * P:t * P + P], mkT[:, h, :],
                                  start=True, stop=True)
                    last.then_inc(lg_made, 1)
                    if u >= 1:
                        pe.wait_ge(y2_done, u)
                    pe.wait_ge(pnorm, u + 1)
                    for m in range(2):
                        for t in range(TPH):
                            last = nc.tensor.transpose(tp[:, m * HALF + t * P:m * HALF + t * P + P],
                                                       prob[:, t, m * P:m * P + P], ident)
                    last.then_inc(p_turned, 1)
                    pe.wait_ge(pT_done, u + 1)
                    for m in range(2):
                        last = mm(tp[:, 0:HALF], mv[:, m, h * P:h * P + P], probT[:, m, :], start=(m == 0), stop=(m == 1))
                    last.then_inc(pv_made, 1)
                elif kind == "wout":
                    _, f, b = step
                    w = need_weights(step, 0)
                    pe.wait_ge(B_free, n_of("B", ("branch", f, BRANCH_ORDER[-1], 3, "br", 1)))
                    for t in range(TPH):
                        r, key = pieces[t]
                        bank = open_piece(r, key)
                        project(r, key, bank[:, 0:WCOLS], lambda k: merged[:, k, t * P:t * P + P], lambda k: w[:, k, :])
                elif kind == "turn":
                    f = step[1]
                    for i, (r, key) in enumerate(pieces):
                        t, g = i // 2, i % 2
                        bank = open_piece(r, key)
                        pe.wait_ge(h2_done, TPH * f + t + 1)
                        for k in range(4):
                            last = nc.tensor.transpose(bank[:, k * P:k * P + P],
                                                       h2[:, TPH * f + t, (4 * g + k) * P:(4 * g + k + 1) * P], ident)
                        last.then_inc(A_full, 1)
                elif kind == "pq":
                    _, f, b = step
                    w = need_weights(step, 0)
                    pe.wait_ge(A_free, n_of("A", ("turn", f, TPH - 1, 1)))
                    pe.wait_ge(late_in, 48)
                    for c in range(2):
                        r, key = pieces[c]
                        bank = open_piece(r, key)
                        project(r, key, bank[:, 0:HALF], lambda k: w[:, k, c * P:c * P + P], lambda k: merged[:, k, :])
                    for c in range(2):
                        hp = 2 * b + c
                        r, key = pieces[2 + c]
                        bank = open_piece(r, key)
                        pe.wait_ge(A_free, n_of(*pieces[c]))
                        for t in range(TPH):
                            last = mm(bank[:, t * P:t * P + P], qpT[:, c, t * P:t * P + P], keys[:, hp * NK:hp * NK + NK],
                                      start=True, stop=True)
                        last.then_inc(A_full, 1)
                elif kind == "open":
                    t = step[1]
                    if t == 0:
                        pe.wait_ge(st_done, 2 * H)
                        pe.sem_inc(used, RING)
                    else:
                        pe.wait_ge(drained, t)
                    for c in range(2):
                        mm(wide[:, 512 * c:512 * c + 512], zeros, keys[:, 0:512], start=True, stop=False,
                           skip_group_check=True)
                elif kind == "gather":
                    _, t, k, n = step
                    whole = n // RING
                    if whole > 1:
                        with pe.Fori(0, whole) as it:
                            for s in range(RING):
                                products(t, k + s, (t * SLOTS + k + s) % RING, it)
                    else:
                        whole = 0
                    for i in range(whole * RING, n):
                        products(t, k + i, (t * SLOTS + k + i) % RING, 0)

        @block.scalar
        def _(act):
            done = [0]
            af = nc.scalar.activation

            def then_wait(ins):
                done[0] += 1
                ins.then_inc(a_ord, 1)
                act.wait_ge(a_ord, done[0])

            def turn_in(r, key):
                act.wait_ge(full[r], n_of(r, key))
                return bank_of(r, key)

            def gather_body(t, k, n, it):
                g = t * SLOTS + k
                for c in range(0, n, GROUP):
                    m = min(GROUP, n - c)
                    act.wait_ge(dot, it * RING + (g + c + m))
                    s = (g + c) % RING
                    af(acts[:, 1, s:s + m], acts[:, 0, s:s + m], ACT.Gelu).then_inc(gel, 1)
                    act.wait_ge(gel, it * (RING // GROUP) + (g + c) // GROUP + 1)
                    for i in range(c, c + m):
                        s = (g + i) % RING
                        col = gate[:, t, k + i:k + i + 1] if isinstance(it, int) else gate[:, t, bass.ds(it * RING + (k + i), 1)]
                        af(acts[:, 2, s:s + 1], acts[:, 1, s:s + 1], ACT.Copy, scale=col).then_inc(wgt, 1)
                    act.wait_ge(wgt, it * RING + (g + c + m))
                    for i in range(c, c + m):
                        s = (g + i) % RING
                        af(diag[:, s, :], ident, ACT.Copy, scale=acts[:, 2, s:s + 1]).then_inc(dia, 1)

            for step in steps:
                kind = step[0]
                pieces = chunks_of(step)
                if kind == "norm_in":
                    act.wait_ge(x_in, 64)
                    for k in range(KD):
                        af(sqx[:, k, :], hT[:, k, :], ACT.Square).then_inc(sq_done, 1)
                    act.wait_ge(mem_in, 16)
                    for k in range(KD):
                        af(sqm[:, k, :], memT[:, k, :], ACT.Square).then_inc(sq_done, 1)
                    act.wait_ge(eps_done, 1)
                    bank = turn_in(*pieces[0])
                    af(bank[:, :], bank[:, :], ACT.Sqrt, scale=1.0 / D, bias=eps[:, :]).then_inc(root, 1)
                    act.wait_ge(h_done, KD)
                    act.sem_inc(A_free, 1)
                elif kind == "norm_mem":
                    bank = turn_in(*pieces[0])
                    af(bank[:, 0:NMEM], bank[:, 0:NMEM], ACT.Sqrt, scale=1.0 / D, bias=eps[:, :]).then_inc(root, 1)
                    act.wait_ge(m_done, KD)
                    act.sem_inc(A_free, 1)
                    act.wait_ge(lb_diff, 2)
                    af(lbs[:, 0:2, :], lbs[:, 0:2, :], ACT.Exp).then_inc(lb_exp, 1)
                elif kind == "kv":
                    for c in range(2):
                        bank = turn_in(*pieces[c])
                        b = step[1]
                        dst = mkT[:, 2 * b + c, :] if b < 2 else mv[:, c, (b - 2) * WCOLS:(b - 1) * WCOLS]
                        af(dst, bank[:, 0:NMEM], ACT.Copy).then_inc(A_free, 1)
                elif kind == "z":
                    _, d, b = step
                    for c in range(2):
                        h = 2 * b + c
                        bank = turn_in(*pieces[c])
                        af(sig[:, d, h, :], bank[:, :], ACT.Sigmoid)
                        af(sgn[:, d, h, :], bank[:, :], ACT.Sigmoid, scale=-1.0).then_inc(A_free, 1)
                elif kind == "q":
                    for c in range(2):
                        bank = turn_in(*pieces[c])
                        af(qT[:, 2 * step[1] + c, :], bank[:, :], ACT.Silu).then_inc(A_free, 1)
                elif kind == "v":
                    for t in range(NT):
                        bank = turn_in(*pieces[t])
                        af(v[:, t, step[1] * WCOLS:(step[1] + 1) * WCOLS], bank[:, 0:WCOLS], ACT.Copy).then_inc(A_free, 1)
                elif kind == "logf":
                    act.wait_ge(lb_done, 1)
                    act.wait_ge(A_free, n_of("A", ("z", 1, 1, 1)))
                    for h in range(H):
                        for d in range(2):
                            u = 4 * d + h
                            af(sig[:, d, h, :], sig[:, d, h, :], ACT.Ln, scale=lbs[:, 1, u:u + 1],
                               bias=lbs[:, 0, u:u + 1]).then_inc(logf_done, 1)
                elif kind == "elem":
                    _, h, d = step
                    u = 2 * h + d
                    act.wait_ge(dsub, 2 * u + 2)
                    af(expn[d][:, :], dref[d][:, :], ACT.Exp, scale=-1.0).then_inc(exps, 1)
                    af(dlast[d][:, :], dlast[d][:, :], ACT.Exp).then_inc(exps, 1)
                    af(cumG[d][:, :], cumG[d][:, :], ACT.Exp).then_inc(exps, 1)
                    act.wait_ge(exps, 4 * u + 1)
                    af(dref[d][:, :], dref[d][:, :], ACT.Exp).then_inc(exps, 1)
                elif kind == "intra":
                    _, h, d = step
                    u = 2 * h + d
                    act.wait_ge(kd_turned, u + 1)
                    act.wait_ge(zero_done, 2)
                    for i in range(2):
                        rows = slice(CH * i, CH * i + CH)
                        last = af(kdn[d][rows, :, i, :], tp[rows, :].rearrange("p (j e) -> p j e", j=NT), ACT.Copy)
                    last.then_inc(kd_copied, 1)
                elif kind == "o":
                    h = step[1]
                    act.wait_ge(o_made, h + 1)
                    af(oT[:, h, :], tp[:, :], ACT.Copy).then_inc(o_kept, 1)
                elif kind == "conv":
                    n = window(step[1])[1]
                    for c in range(2):
                        bank = turn_in(*pieces[c])
                        g = (step[1] * 2 + step[2]) * 2 + c
                        if step[1]:
                            act.wait_ge(y0_done, H * step[1])
                        if g >= 2:
                            act.wait_ge(y1_done, g - 1)
                        af(csb[:, c, 0:n], bank[:, 0:n], ACT.Copy).then_inc(A_free, 1)
                elif kind == "mq":
                    for c in range(2):
                        bank = turn_in(*pieces[c])
                        if step[1] >= 1:
                            act.wait_ge(top1_done, 4 * TPH * step[1])
                        af(mqT[:, 2 * step[2] + c, :], bank[:, 0:HALF], ACT.Copy).then_inc(A_free, 1)
                elif kind == "att":
                    _, f, h = step
                    u = H * f + h
                    act.wait_ge(mx_done, u + 1)
                    if u >= 1:
                        act.wait_ge(p_turned, u)
                    for t in range(TPH):
                        af(prob[:, t, :], scb[:, t * NMEM:(t + 1) * NMEM], ACT.Exp, scale=float(P) ** -0.5,
                           bias=tiny[:, t:t + 1], accum_out=tiny[:, 4 + t:5 + t]).then_inc(pexp, 1)
                    act.wait_ge(p_turned, u + 1)
                    if u >= 1:
                        act.wait_ge(pv_made, u)
                    af(probT, tp[:, :].rearrange("p (m t) -> p m t", m=2), ACT.Copy).then_inc(pT_done, 1)
                    act.wait_ge(pv_made, u + 1)
                    af(y[2][:, h, :], tp[:, 0:HALF], ACT.Copy).then_inc(y2_done, 1)
                elif kind == "branch":
                    _, f, n, b = step
                    for c in range(2):
                        r, key = pieces[2 * c]
                        bank = turn_in(r, key)
                        before = [k for k in order["B"][:place["B"][pieces[2 * c + 1][1]]] if k[0] == "branch"][-2:]
                        if len(before) == 2:
                            act.wait_ge(B_free, n_of("B", before[0]))
                        if n == 0:
                            act.wait_ge(y0_done, H * (f + 1))
                        af(gsb[:, c, :], bank[:, 0:HALF], ACT.Sigmoid).then_inc(A_free, 1)
                elif kind == "hg":
                    _, f, b = step
                    if f or b:
                        act.wait_ge(y0_done, f * H + 2 * b)
                    for c in range(2):
                        h = 2 * b + c
                        act.wait_ge(o_kept, H)
                        act.wait_ge(B_free, n_of("B", last_before_hg[f]))
                        af(tmp[:, c, :], oT[:, h, f * HALF:(f + 1) * HALF], ACT.Square).then_inc(osq_done, 1)
                    for c in range(2):
                        bank = turn_in(*pieces[2 * c])
                        af(csb[:, c, 0:HALF], bank[:, 0:HALF], ACT.Silu).then_inc(A_free, 1)
                        bank = turn_in(*pieces[2 * c + 1])
                        af(gsb[:, c, :], bank[:, 0:HALF], ACT.Sqrt, scale=1.0 / P, bias=eps[:, :]).then_inc(A_free, 1)
                elif kind == "ffn":
                    f = step[1]
                    for t in range(TPH):
                        act.wait_ge(B_free, n_of("B", ("wout", f, 3, TPH - 1)))
                        then_wait(af(junk[:, :], x2[:, t, :], ACT.Square, accum_out=tiny[:, 8 + t:9 + t]))
                        af(tiny[:, 10 + t:11 + t], tiny[:, 8 + t:9 + t], ACT.Sqrt, scale=1.0 / D,
                           bias=eps[:, :]).then_inc(ssq_done, 1)
                elif kind == "turn":
                    f = step[1]
                    for i, (r, key) in enumerate(pieces):
                        t, g = i // 2, i % 2
                        bank = turn_in(r, key)
                        af(merged[:, 4 * g:4 * g + 4, t * P:t * P + P], bank[:, :].rearrange("p (k t) -> p k t", k=4),
                           ACT.Copy).then_inc(A_free, 1)
                elif kind == "pq":
                    _, f, b = step
                    for c in range(2):
                        bank = turn_in(*pieces[c])
                        if b or f:
                            prev = ("pq", f, b - 1, "s", c) if b else ("pq", f - 1, HP // 2 - 1, "s", c)
                            act.wait_ge(A_full, n_of("A", prev))
                        af(qpT[:, c, :], bank[:, 0:HALF], ACT.Copy).then_inc(A_free, 1)
                    for c in range(2):
                        hp = 2 * b + c
                        bank = turn_in(*pieces[2 + c])
                        af(score[:, :, hp * NK:hp * NK + NK], bank[:, 0:TPH * P].rearrange("p (t k) -> p t k", t=TPH),
                           ACT.Copy).then_inc(A_free, 1)
                elif kind == "gate":
                    t = step[1]
                    act.wait_ge(gd_done, t + 1)
                    af(bs[:, :, :], bs[:, :, :], ACT.Exp).then_inc(ge_done, 1)
                elif kind == "open":
                    act.wait_ge(gate_done, step[1] + 1)
                elif kind == "gather":
                    _, t, k, n = step
                    whole = n // RING
                    if whole > 1:
                        with act.Fori(0, whole) as it:
                            gather_body(t, k, RING, it)
                    else:
                        whole = 0
                    if n > whole * RING:
                        gather_body(t, k + whole * RING, n - whole * RING, 0)
                elif kind == "drain":
                    t = step[1]
                    act.wait_ge(x2_kept, 16 * TPH * (t // TPH + 1))
                    act.wait_ge(dot, (t + 1) * SLOTS)
                    act.dma_start(h2[:, t, :], x2n[t]).then_inc(back_in, 16)
                elif kind == "last":
                    t = step[1]
                    act.wait_ge(drained, t + 1)
                    then_wait(af(junk[:, :], h2[:, t, :], ACT.Square, accum_out=tiny[:, 16:17]))
                    af(tiny[:, 17:18], tiny[:, 16:17], ACT.Sqrt, scale=1.0 / D, bias=eps[:, :]).then_inc(fsq, 1)
                    act.wait_ge(fdone, t + 1)
                    act.dma_start(outn[t], h2[:, t, :]).then_inc(out_done, 16)
            act.wait_ge(out_done, 16 * NT)

        @block.vector
        def _(dve):
            done = [0]
            ve = nc.vector

            def tick(ins):
                done[0] += 1
                ins.then_inc(v_ord, 1)

            def settle():
                dve.wait_ge(v_ord, done[0])

            def link(ins):
                tick(ins)
                settle()

            def turn_in(r, key):
                dve.wait_ge(full[r], n_of(r, key))
                return bank_of(r, key)

            def dots(t, k, n, it):
                for i in range(n):
                    g = t * SLOTS + k + i
                    s = g % RING
                    dve.wait_ge(landed[s], it * 16 + land_count(g))
                    ve.tensor_tensor_reduce(ring[:, s, 0:D], ring[:, s, 0:D], h2[:, t, :], 1.0, 0.0, ALU.mult, ALU.add,
                                            acts[:, 0, s:s + 1]).then_inc(dot, 1)

            for step in steps:
                kind = step[0]
                pieces = chunks_of(step)
                if kind == "norm_in":
                    dve.wait_ge(c_in, 48)
                    l0, l1 = vec[:, V_LB:V_LB + 8], vec[:, V_LB + 8:V_LB + 16]
                    ve.memset(eps[:, :], EPS).then_inc(eps_done, 1)
                    link(ve.tensor_tensor(lbs[:, 2, :], l0, l1, ALU.max))
                    ve.tensor_tensor(lbs[:, 0, :], l0, lbs[:, 2, :], ALU.subtract).then_inc(lb_diff, 1)
                    ve.tensor_tensor(lbs[:, 1, :], l1, lbs[:, 2, :], ALU.subtract).then_inc(lb_diff, 1)
                elif kind == "norm_mem":
                    pass
                if kind in ("norm_in", "norm_mem"):
                    src_t, n, g0, dn = (hT, T, V_MIX, h_done) if kind == "norm_in" else (memT, NMEM, V_MEM, m_done)
                    r, key = pieces[0]
                    bank = turn_in(r, key)
                    dve.wait_ge(root, n_of(r, key))
                    link(ve.reciprocal(bank[:, 0:n], bank[:, 0:n]))
                    for k in range(KD):
                        last = ve.scalar_tensor_tensor(out=src_t[:, k, :], in0=src_t[:, k, :], scalar=vec[:, g0 + k:g0 + k + 1],
                                                       in1=bank[:, 0:n], op0=ALU.mult, op1=ALU.mult)
                        last.then_inc(dn, 1)
                elif kind == "kv" and step[1] == 0:
                    dve.wait_ge(lb_exp, 1)
                    link(ve.tensor_tensor(lbs[:, 2, :], lbs[:, 0, :], lbs[:, 1, :], ALU.add))
                    link(ve.reciprocal(lbs[:, 2, :], lbs[:, 2, :]))
                    link(ve.tensor_tensor(lbs[:, 0, :], lbs[:, 0, :], lbs[:, 2, :], ALU.mult))
                    ve.tensor_scalar(lbs[:, 1, :], lbs[:, 0, :], -1.0, 1.0, ALU.mult, ALU.add).then_inc(lb_done, 1)
                    for d in range(2):
                        tick(ve.memset(PT[d][:, :], 0.0))
                    for d in range(2):
                        ve.memset(kdn[d][:, :, :, :], 0.0).then_inc(zero_done, 1)
                    ve.memset(ub[:, :, :], 0.0).then_inc(zero_done, 1)
                elif kind == "elem":
                    _, h, d = step
                    u = 2 * h + d
                    dve.wait_ge(logf_done, u + 1)
                    dve.wait_ge(A_free, n_of("A", ("q", 1, 1)))
                    if h >= 1:
                        dve.wait_ge(o_made, h)
                    lf = sig[:, d, h, :]
                    G = cumG[d]
                    if d == 0:
                        link(ve.tensor_tensor_scan(G[:, :], hcst[:, S_KEEP:S_KEEP + T], lf, 0.0, ALU.mult, ALU.add))
                    else:
                        link(ve.tensor_tensor_scan(G[:, ::-1], hcst[:, S_KEEP:S_KEEP + T], lf[:, ::-1], 0.0, ALU.mult, ALU.add))
                    mid, end = (CH // 2 - 1, CH - 1) if d == 0 else (CH // 2, 0)
                    Gc = G[:, :].rearrange("p (n c) -> p n c", c=CH)
                    ve.tensor_tensor(dref[d][:, :].rearrange("p (n c) -> p n c", c=CH), Gc,
                                     Gc[:, :, mid:mid + 1].to_broadcast([P, NCH, CH]), ALU.subtract).then_inc(dsub, 1)
                    ve.tensor_tensor(dlast[d][:, :].rearrange("p (n c) -> p n c", c=CH),
                                     Gc[:, :, end:end + 1].to_broadcast([P, NCH, CH]), Gc, ALU.subtract).then_inc(dsub, 1)
                    lb1 = lbs[:, 1, 4 * d + h:4 * d + h + 1]
                    k_ = sgn[:, d, h, :]
                    dve.wait_ge(exps, 4 * u + 1)
                    ve.scalar_tensor_tensor(out=expn[d][:, :], in0=k_, scalar=lb1, in1=expn[d][:, :],
                                            op0=ALU.mult, op1=ALU.mult).then_inc(prods, 1)
                    dve.wait_ge(exps, 4 * u + 2)
                    ve.scalar_tensor_tensor(out=dlast[d][:, :], in0=k_, scalar=lb1, in1=dlast[d][:, :],
                                            op0=ALU.mult, op1=ALU.mult).then_inc(prods, 1)
                    dve.wait_ge(exps, 4 * u + 4)
                    tick(ve.tensor_copy(decay[d][:, :], Gc[:, :, end]))
                    ve.tensor_tensor(dref[d][:, :], dref[d][:, :], qT[:, h, :], ALU.mult).then_inc(prods, 1)
                    settle()
                    ve.tensor_tensor(G[:, :], G[:, :], qT[:, h, :], ALU.mult).then_inc(prods, 1)
                elif kind == "intra":
                    _, h, d = step
                    u = 2 * h + d
                    dve.wait_ge(sc_made, u + 1)
                    settle()
                    m = hcst[:, (S_MF, S_MB)[d]:(S_MF, S_MB)[d] + P].bitcast(U32)
                    ve.copy_predicated(PT[d][:, :].rearrange("p (j t) -> p j t", j=NT),
                                       m.unsqueeze(1).to_broadcast([P, NT, P]),
                                       scb[:, :].rearrange("p (j t) -> p j t", j=NT)).then_inc(sc_masked, 1)
                    dve.wait_ge(ds_made, u + 1)
                    seq = list(range(NCH)) if d == 0 else list(range(NCH - 1, -1, -1))
                    st = state[d]
                    for i in range(NCH - 1):
                        n, nx = seq[i], seq[i + 1]
                        dS = wide[:, n * P:n * P + P]
                        if i == 0:
                            ins = ve.tensor_copy(st[:, nx, :], dS)
                        else:
                            ins = ve.scalar_tensor_tensor(out=st[:, nx, :], in0=st[:, n, :], scalar=decay[d][:, n:n + 1],
                                                          in1=dS, op0=ALU.mult, op1=ALU.add)
                        if i < NCH - 2:
                            link(ins)
                        else:
                            ins.then_inc(st_done, 1)
                elif kind == "conv":
                    _, f, b = step
                    t0, n, c0 = window(f)
                    for c in range(2):
                        bank = turn_in(*pieces[2 + c])
                        dve.wait_ge(zero_done, 3)
                        dve.wait_ge(A_free, n_of(*pieces[c]))
                        if f == 1 and b == 0:
                            link(ve.memset(ub[:, c, HALF + 1:HALF + 2], 0.0))
                        ve.tensor_tensor(ub[:, c, c0:c0 + n], csb[:, c, 0:n], bank[:, 0:n], ALU.mult).then_inc(B_free, 1)
                    for c in range(2):
                        ch = 2 * b + c
                        dve.wait_ge(B_free, n_of(*pieces[2 + c]))
                        w = [vec[:, V_CONV + 4 * j + ch:V_CONV + 4 * j + ch + 1] for j in range(3)]
                        yc = y[1][:, ch, :]
                        if f == 1 and ch == 0:
                            settle()
                        link(ve.tensor_scalar(yc, ub[:, c, 0:HALF], w[0], None, ALU.mult))
                        for j in (1, 2):
                            link(ve.scalar_tensor_tensor(out=yc, in0=ub[:, c, j:j + HALF], scalar=w[j], in1=yc,
                                                         op0=ALU.mult, op1=ALU.add))
                        bank = turn_in(*pieces[4 + c])
                        link(ve.tensor_tensor(yc, yc, bank[:, 0:HALF], ALU.mult))
                        dve.sem_inc(B_free, 1)
                        dve.sem_inc(y1_done, 1)
                elif kind == "att":
                    _, f, h = step
                    u = H * f + h
                    dve.wait_ge(lg_made, u + 1)
                    link(ve.tensor_reduce(tiny[:, 2:4], scb[:, :].rearrange("p (t m) -> p t m", t=TPH), AX_X, ALU.max))
                    if u:
                        dve.wait_ge(pexp, TPH * u)
                    ve.tensor_scalar(tiny[:, 0:2], tiny[:, 2:4], -float(P) ** -0.5, None, ALU.mult).then_inc(mx_done, 1)
                    dve.wait_ge(pexp, TPH * (u + 1))
                    link(ve.reciprocal(tiny[:, 6:8], tiny[:, 4:6]))
                    for t in range(TPH):
                        ins = ve.tensor_scalar(prob[:, t, :], prob[:, t, :], tiny[:, 6 + t:7 + t], None, ALU.mult)
                        tick(ins) if t == 0 else ins.then_inc(pnorm, 1)
                elif kind == "branch":
                    _, f, n, b = step
                    for c in range(2):
                        dc = 2 * b + c
                        dve.wait_ge(A_free, n_of(*pieces[2 * c]))
                        bank = turn_in(*pieces[2 * c + 1])
                        if n == BRANCH_ORDER[0]:
                            ve.tensor_tensor(merged[:, dc, :], gsb[:, c, :], bank[:, 0:HALF], ALU.mult).then_inc(B_free, 1)
                        else:
                            link(ve.tensor_tensor(gsb[:, c, :], gsb[:, c, :], bank[:, 0:HALF], ALU.mult))
                            ve.tensor_tensor(merged[:, dc, :], merged[:, dc, :], gsb[:, c, :], ALU.add).then_inc(B_free, 1)
                elif kind == "hg":
                    _, f, b = step
                    for c in range(2):
                        h = 2 * b + c
                        dve.wait_ge(A_free, n_of(*pieces[2 * c + 1]))
                        link(ve.reciprocal(gsb[:, c, :], gsb[:, c, :]))
                        link(ve.scalar_tensor_tensor(out=gsb[:, c, :], in0=oT[:, h, f * HALF:(f + 1) * HALF],
                                                     scalar=vec[:, V_HG + h:V_HG + h + 1], in1=gsb[:, c, :],
                                                     op0=ALU.mult, op1=ALU.mult))
                        ve.tensor_tensor(y[0][:, h, :], gsb[:, c, :], csb[:, c, 0:HALF], ALU.mult).then_inc(y0_done, 1)
                elif kind == "wout":
                    _, f, b = step
                    for t in range(TPH):
                        bank = turn_in(*pieces[t])
                        dve.wait_ge(x_nat, 16 * TPH * (f + 1))
                        cols = slice(b * WCOLS, (b + 1) * WCOLS)
                        ve.tensor_tensor(x2[:, t, cols], x2[:, t, cols], bank[:, 0:WCOLS], ALU.add).then_inc(B_free, 1)
                elif kind == "ffn":
                    f = step[1]
                    dve.wait_ge(late_in, 48)
                    for t in range(TPH):
                        dve.wait_ge(ssq_done, TPH * f + t + 1)
                        link(ve.reciprocal(tiny[:, 12 + t:13 + t], tiny[:, 10 + t:11 + t]))
                        ve.scalar_tensor_tensor(out=h2[:, TPH * f + t, :], in0=x2[:, t, :], scalar=tiny[:, 12 + t:13 + t],
                                                in1=g_ffn[:, :], op0=ALU.mult, op1=ALU.mult).then_inc(h2_done, 1)
                elif kind == "top1":
                    _, t, grp = step
                    f, tl = t // TPH, t % TPH
                    dve.wait_ge(A_free, n_of("A", ("pq", f, HP // 2 - 1, "s", 1)))
                    hps = range(4 * grp, 4 * grp + 4)
                    sc_ = lambda hp: score[:, tl, hp * NK:hp * NK + NK]
                    settle()
                    for hp in hps:
                        tick(ve.max(tv[:, hp, 0:8], sc_(hp)))
                    settle()
                    for hp in hps:
                        tick(ve.max_index(ti[:, hp, 0:8], tv[:, hp, 0:8], sc_(hp)))
                    settle()
                    for hp in hps:
                        tick(ve.match_replace(sc_(hp), tv[:, hp, 0:8], sc_(hp), NEG))
                    settle()
                    for hp in hps:
                        tick(ve.max(tv[:, hp, 8:16], sc_(hp)))
                    settle()
                    for hp in hps:
                        tick(ve.max_index(ti[:, hp, 8:16], tv[:, hp, 8:16], sc_(hp)))
                    settle()
                    dve.sem_inc(top1_done, 1)
                elif kind == "top2":
                    settle()
                    link(ve.tensor_copy(tif[:, :, :], ti[:, :, :]))
                    tif4 = tif[:, :, :].rearrange("p (h s) k -> p h s k", s=2)
                    tv4 = tv[:, :, :].rearrange("p (h s) k -> p h s k", s=2)
                    link(ve.tensor_scalar(tif4[:, :, 0, :], tif4[:, :, 0, :], float(NK), None, ALU.mult))
                    for dst, s4 in ((cs, tv4), (ci, tif4)):
                        off = 0
                        for i0, ni, nj in CAND_ROWS:
                            o_ = dst[:, :, off:off + ni * nj].rearrange("p h (i j) -> p h i j", i=ni)
                            tick(ve.tensor_tensor(o_, s4[:, :, 0, i0:i0 + ni].unsqueeze(3).to_broadcast([P, PH, ni, nj]),
                                                  s4[:, :, 1, 0:nj].unsqueeze(2).to_broadcast([P, PH, ni, nj]), ALU.add))
                            off += ni * nj
                elif kind == "top3":
                    _, t, grp = step
                    hs = range(4 * grp, 4 * grp + 4)
                    settle()
                    for h in hs:
                        tick(ve.max(bs[:, h, 0:8], cs[:, h, :]))
                    settle()
                    for h in hs:
                        tick(ve.max_index(pos[:, h, 0:8], bs[:, h, 0:8], cs[:, h, :]))
                    settle()
                    for h in hs:
                        tick(ve.match_replace(cs[:, h, :], bs[:, h, 0:8], cs[:, h, :], NEG))
                    settle()
                    for h in hs:
                        tick(ve.max(bs[:, h, 8:16], cs[:, h, :]))
                    settle()
                    for h in hs:
                        tick(ve.max_index(pos[:, h, 8:16], bs[:, h, 8:16], cs[:, h, :]))
                elif kind == "look":
                    _, t, grp = step
                    if grp == 0:
                        settle()
                        link(ve.tensor_copy(posf[:, :, :], pos[:, :, :]))
                    iota = cst[:, C_IOTA:C_IOTA + NCAND].unsqueeze(1).to_broadcast([P, TOP, NCAND])
                    for h in range(4 * grp, 4 * grp + 4):
                        link(ve.tensor_tensor(eq[:, :, :], iota, posf[:, h, :].unsqueeze(2).to_broadcast([P, TOP, NCAND]),
                                              ALU.is_equal))
                        link(ve.tensor_tensor(eq[:, :, :], eq[:, :, :], ci[:, h, :].unsqueeze(1).to_broadcast([P, TOP, NCAND]),
                                              ALU.mult))
                        link(ve.tensor_reduce(posf[:, h, :], eq[:, :, :], AX_X, ALU.add))
                    if grp == 1:
                        ve.tensor_copy(idx[:, t, :], posf[:, :, :].rearrange("p h k -> p (h k)")).then_inc(idx_done, 1)
                elif kind == "gate":
                    t = step[1]
                    settle()
                    link(ve.tensor_copy(tiny[:, 24:32], bs[:, :, 0]))
                    ve.tensor_tensor(bs[:, :, :], bs[:, :, :], tiny[:, 24:32].unsqueeze(2).to_broadcast([P, PH, TOP]),
                                     ALU.subtract).then_inc(gd_done, 1)
                    dve.wait_ge(ge_done, t + 1)
                    link(ve.tensor_reduce(tiny[:, 24:32], bs[:, :, :], AX_X, ALU.add))
                    link(ve.reciprocal(tiny[:, 24:32], tiny[:, 24:32]))
                    ve.tensor_tensor(gate[:, t, :].rearrange("p (h k) -> p h k", h=PH), bs[:, :, :],
                                     tiny[:, 24:32].unsqueeze(2).to_broadcast([P, PH, TOP]), ALU.mult).then_inc(gate_done, 1)
                elif kind == "gather":
                    _, t, k, n = step
                    whole = n // RING
                    if whole > 1:
                        with dve.Fori(0, whole) as it:
                            dots(t, k, RING, it)
                    else:
                        whole = 0
                    dots(t, k + whole * RING, n - whole * RING, 0)
                elif kind == "drain":
                    t = step[1]
                    dve.wait_ge(back_in, 16 * (t + 1))
                    dve.wait_ge(used, RING + (t + 1) * SLOTS)
                    ve.tensor_tensor(h2[:, t, :], h2[:, t, :], wide[:, :], ALU.add).then_inc(drained, 1)
                elif kind == "last":
                    t = step[1]
                    dve.wait_ge(fsq, t + 1)
                    link(ve.reciprocal(tiny[:, 18:19], tiny[:, 17:18]))
                    ve.scalar_tensor_tensor(out=h2[:, t, :], in0=h2[:, t, :], scalar=tiny[:, 18:19], in1=g_fin[:, :],
                                            op0=ALU.mult, op1=ALU.mult).then_inc(fdone, 1)


def kernel(**inp):
    import numpy as _np
    import concourse.bacc as _bacc
    from concourse.bass_utils import run_bass_kernel_spmd as _run

    def cols(v_):
        return _np.asarray(v_).reshape(-1, P).T

    g = {k: _np.asarray(v_) for k, v_ in inp.items()}
    vec = _np.concatenate([cols(g["norm_mix_g"][0]), cols(g["mem_norm_g"][0]), cols(g["hg_lb"][0].reshape(-1)),
                           cols(g["hg_lb"][1].reshape(-1)), cols(g["hg_norm_g"][0]), cols(g["sc_conv_w"][0].reshape(-1))], axis=1)
    arrays = {
        "xT": g["x"][0].T, "x": g["x"][0], "memT": g["mem"][0].T, "cst": constants()[0], "hcst": constants()[1], "vec": vec,
        "w_in": g["w_in"][0], "w_kv": g["w_mem_kv"][0], "w_br": g["w_branch"][0].reshape(3 * BW, D),
        "w_out": g["w_out"][0], "w_pq": g["peer_w_q"][0],
        "keys": g["peer_sub_keys"][0].reshape(HP, NK, P).transpose(2, 0, 1).reshape(P, HP * NK),
        "g_ffn": _np.broadcast_to(g["norm_ffn_g"][0], (P, D)), "g_fin": _np.broadcast_to(g["final_norm_g"], (P, D)),
        "uv": _np.concatenate([g["peer_u"][0], g["peer_v"][0]], axis=1),
    }
    arrays = {k: _np.ascontiguousarray(v_) for k, v_ in arrays.items()}
    nc = _bacc.Bacc("TRN2", target_bir_lowering=False, num_devices=1)
    args = {k: nc.dram_tensor(f"in_{k}", v_.shape, F32, kind="ExternalInput").ap() for k, v_ in arrays.items()}
    out = nc.dram_tensor("out_y", (1, T, D), F32, kind="ExternalOutput").ap()
    build(nc, args, out)
    r = _run(nc, [{f"in_{k}": v_ for k, v_ in arrays.items()}], core_ids=[0])
    return r.results[0]["out_y"]
```

```python
from contextlib import ExitStack

import numpy as np

import concourse.bass as bass
from concourse import mybir

F32 = mybir.dt.float32
U32 = mybir.dt.uint32
BF16 = mybir.dt.bfloat16
ALU = mybir.AluOpType
ACT = mybir.ActivationFunctionType
AX_X = mybir.AxisListType.X

P = 128
T = 512
D = 1024
KD = D // P
NT = T // P
HALF = 256
TPH = HALF // P
HALVES = T // HALF
NMEM = 256
H = 4
CH = 64
NCH = T // CH
BW = 512
BC = BW // P
EPS = 1e-6
NEG = -3.0e38
HP = 16
PH = 8
NK = 128
TOP = 16
SLOTS = PH * TOP
RING = 6
GROUP = 2
QH = 4
HQ = PH // QH
SHARE = {"best": 5.0, "look": 4.0, "conv": 7.5, "mq": 5.0, "branch": 7.5, "att": 4.5, "hg": 7.0, "wout": 5.0, "ffn": 2.0,
         "turn": 3.0, "pq": 6.0}
WSLOTS = 4
WCOLS = 256
CAND_ROWS = ((0, 1, 16), (1, 1, 8), (2, 1, 5), (3, 1, 4), (4, 4, 3), (8, 8, 1))
NCAND = sum(ni * nj for _, ni, nj in CAND_ROWS)
COL_Q, COL_V, COL_F, COL_B, COL_HG, COL_SB, COL_SC, COL_SH, COL_MQ, COL_GATE = (BW * i for i in range(10))
C_ID, C_ONE, C_ZERO, C_IOTA = 0, 128, 256, 384
C_N = C_IOTA + NCAND
S_MF, S_MB, S_KEEP = 0, 128, 256
S_N = S_KEEP + T
V_MIX, V_MEM, V_LB, V_HG, V_CONV = 0, 8, 16, 32, 36
V_N = 48
BRANCH_ORDER = (1, 2, 0)


def constants():
    c, m = np.zeros((P, C_N), np.float32), np.zeros((P, S_N), np.float32)
    c[:, C_ID:C_ID + P] = np.eye(P)
    c[:, C_ONE:C_ONE + P] = 1.0
    s, t = np.arange(P)[:, None], np.arange(P)[None, :]
    same = s // CH == t // CH
    m[:, S_MF:S_MF + P] = same & (s <= t)
    m[:, S_MB:S_MB + P] = same & (s >= t)
    m[:, S_KEEP:S_KEEP + T] = np.arange(T) % CH != 0
    c[:, C_IOTA:] = np.arange(NCAND)
    return c, m


def plan():
    steps = [("norm_mem",), ("norm_in",)]
    steps += [("kv", b) for b in range(4)]
    steps += [("z", d, b) for d in range(2) for b in range(2)]
    steps += [("q", b) for b in range(2)] + [("v", b) for b in range(2)]

    def mixers(f):
        conv = [("conv", f, b, c) for b in range(2) for c in range(2)]
        mq = [("mq", f, b) for b in range(2)]
        att = [("att", f, h) for h in range(H)]
        br = {n: [("branch", f, n, b) for b in range(4)] for n in range(3)}
        return conv, mq, att, br

    def tail(f):
        return [("hg", f, b) for b in range(2)], [("wout", f, b) for b in range(4)] + [("ffn", f), ("turn", f)]

    def topk(t, g):
        return [("best", t, g), ("look", t, g)]

    conv, mq, att, br = mixers(0)
    side = conv + mq + br[1]
    for s in [("logf",)] + [s for h in range(H) for s in (("elem", h, 0), ("elem", h, 1), "side", "side", ("intra", h, 0),
                                                          "side", ("intra", h, 1), ("o", h))]:
        if s != "side":
            steps.append(s)
        elif side:
            steps.append(side.pop(0))
    hg, end = tail(0)
    steps += side + att + br[2] + hg + br[0] + end
    steps.append(("open", 0))
    first = [("pq", 0, 0), ("pq", 0, 1)] + topk(0, 0)
    for g in range(1, QH):
        first += [("pq", 0, 2 * g), ("pq", 0, 2 * g + 1)] + topk(0, g)

    conv, mq, att, br = mixers(1)
    hg, end = tail(1)
    rest = [s for g in range(QH) for s in topk(1, g)] + conv + mq + br[1] + att + br[2] + hg + br[0] + end
    for g in range(QH):
        rest += [("pq", 1, 2 * g), ("pq", 1, 2 * g + 1)] + topk(2, g)
    late = [s for g in range(QH) for s in topk(3, g)]
    steps += first[:4]
    first = first[4:]
    slot, done = 0, 0.0

    def gather(n):
        nonlocal slot
        while n > 0:
            t, k = divmod(slot, SLOTS)
            m = min(n, SLOTS - k)
            steps.append(("gather", t, k, m))
            slot, n = slot + m, n - m
            if k + m == SLOTS:
                steps.extend([("drain", t), ("last", t)] + ([("open", t + 1)] if t + 1 < NT else []))

    for s in first:
        gather(4 if s[0] == "pq" else 0)
        steps.append(s)
    whole, start = sum(SHARE[s[0]] for s in rest), slot
    for s in rest:
        done += SHARE[s[0]]
        n = round(done / whole * (TPH * SLOTS - 4 - start)) + start - slot
        gather(min(n - n % 2, RING))
        steps.append(s)
    gather(TPH * SLOTS - slot)
    for s in late:
        gather(SLOTS // (2 * QH))
        steps.append(s)
    while slot < NT * SLOTS:
        gather(SLOTS - slot % SLOTS)
    return steps


def tensor_order(steps):
    steps = list(steps)
    for i in range(len(steps) - 1):
        a, b = steps[i:i + 2]
        if a[0] == "gather" and a[3] <= RING and chunks_of(b):
            steps[i:i + 2] = b, a
    return steps


def chunks_of(step):
    k = step[0]
    if k in ("norm_in", "norm_mem"):
        return [("A", step)]
    if k == "kv":
        return [("A", (*step, c)) for c in range(2)]
    if k in ("z", "q"):
        return [("A", (*step, c)) for c in range(2)]
    if k == "v":
        return [("A", (*step, t)) for t in range(NT)]
    if k == "conv":
        return [("A", (*step, "C")), ("B", (*step, "h")), ("B", (*step, "B"))]
    if k == "mq":
        return [("A", (*step, c)) for c in range(2)]
    if k == "branch":
        return [(r, (*step, w, c)) for c in range(2) for r, w in (("A", "gate"), ("B", "br"))]
    if k == "hg":
        return [("A", (*step, w, c)) for c in range(2) for w in ("z", "ss")]
    if k == "wout":
        return [("B", (*step, t)) for t in range(TPH)]
    if k == "turn":
        return [("A", (*step, t, g)) for t in range(TPH) for g in range(2)]
    if k == "pq":
        return [("A", (*step, "q", 0)), ("A", (*step, "q", 1)), ("A", (*step, "s", 0)), ("A", (*step, "s", 1))]
    return []


def weights_of(step):
    k = step[0]
    if k == "kv":
        return [("kv", 0, D, WCOLS * step[1], WCOLS)]
    if k == "z":
        return [("in", 0, D, (COL_F, COL_B)[step[1]] + WCOLS * step[2], WCOLS)]
    if k == "q":
        return [("in", 0, D, COL_Q + WCOLS * step[1], WCOLS)]
    if k == "v":
        return [("in", 0, D, COL_V + WCOLS * step[1], WCOLS)]
    if k == "conv" and step[3] == 0:
        return [("in", 0, D, c + WCOLS * step[2], WCOLS) for c in (COL_SC, COL_SH, COL_SB)]
    if k == "mq":
        return [("in", 0, D, COL_MQ + WCOLS * step[2], WCOLS)]
    if k == "hg":
        return [("in", 0, D, COL_HG + WCOLS * step[2], WCOLS)]
    if k == "branch":
        _, _, n, b = step
        return [("in", 0, D, COL_GATE + D * n + WCOLS * b, WCOLS), ("br", BW * n, BW, WCOLS * b, WCOLS)]
    if k == "wout":
        return [("out", 0, D, WCOLS * step[2], WCOLS)]
    if k == "pq":
        return [("pq", 0, D, WCOLS * step[2], WCOLS)]
    return []


def build(nc, a, out):
    steps = plan()
    order = {"A": [], "B": []}
    last_piece = {}
    blocks, block_of = [], {}
    for s in steps:
        for r, key in chunks_of(s):
            order[r].append(key)
            last_piece[s] = (r, key)
            if s[0] == "conv" and s[3]:
                last_piece[s[:3] + (0,)] = (r, key)
        for i, w in enumerate(weights_of(s)):
            block_of[s, i] = len(blocks)
            blocks.append((s, w))
    place = {r: {key: i for i, key in enumerate(o)} for r, o in order.items()}

    with ExitStack() as ctx:
        def sb(name, shape, dt=F32):
            return ctx.enter_context(nc.sbuf_tensor(name, shape, dt))

        def sem(name):
            return ctx.enter_context(nc.semaphore(name))

        cst = sb("cst", [P, C_N])
        ident, ones, zeros = cst[:, C_ID:C_ID + P], cst[:, C_ONE:C_ONE + P], cst[:, C_ZERO:C_ZERO + P]
        vec = sb("vec", [P, V_N])
        lbs = sb("lbs", [P, 3, 8])
        eps = sb("eps", [P, 1])
        keys = sb("keys", [P, HP * NK])
        g_ffn = sb("g_ffn", [P, D])
        g_fin = sb("g_fin", [P, D])
        hT = sb("hT", [P, KD, T])
        W = sb("W", [P, WSLOTS, KD * WCOLS])
        mkT = sb("mkT", [P, H, NMEM])
        mv = sb("mv", [P, NMEM // P, BW])
        oT = sb("oT", [P, H, T])
        ys = sb("ys", [P, 4096])
        y = [ys[:, n * BC * HALF:(n + 1) * BC * HALF].rearrange("p (c t) -> p c t", c=BC) for n in range(3)]
        score = ys[:, :].rearrange("p (t k) -> p t k", t=TPH)
        mx = sb("mx", [P, KD * HALF])
        merged = mx[:, :].rearrange("p (k t) -> p k t", k=KD)
        mqT = y[2]
        prob = ys[:, 3 * BC * HALF:3 * BC * HALF + 512].rearrange("p (t m) -> p t m", t=TPH)
        probT = ys[:, 3 * BC * HALF + 512:4096].rearrange("p (m t) -> p m t", m=2)
        WIN = HALF + 1
        csb = sb("csb", [P, 2, WIN])
        ub = sb("ub", [P, 2, HALF + 2])
        gsb = sb("gsb", [P, 2, HALF])
        tmp = sb("tmp", [P, 2, HALF])
        qpT = sb("qpT", [P, 2, HALF])
        tiny = sb("tiny", [P, 32])
        acts = sb("acts", [P, 3, RING])
        stage = sb("stage", [P, RING, 1], U32)
        diag = sb("diag", [P, RING, P])
        junk = qpT[:, :, :].rearrange("p c t -> p (c t)").bitcast(BF16)
        AR = RING * 2 * D + NT * D + TPH * D + 3 * HP * TOP + 2 * PH * NCAND + 3 * SLOTS + TOP * NCAND + 2 * NT * SLOTS
        arena = sb("arena", [P, AR])
        at = [0]

        def cut(n):
            at[0] += n
            assert at[0] <= AR, at[0]
            return arena[:, at[0] - n:at[0]]

        sig = cut(2 * H * T).rearrange("p (d h t) -> p d h t", d=2, h=H)
        sgn = cut(2 * H * T).rearrange("p (d h t) -> p d h t", d=2, h=H)
        sqx = arena[:, 0:KD * T].rearrange("p (k t) -> p k t", k=KD)
        memT = arena[:, KD * T:KD * T + KD * NMEM].rearrange("p (k t) -> p k t", k=KD)
        sqm = arena[:, KD * T + KD * NMEM:KD * T + 2 * KD * NMEM].rearrange("p (k t) -> p k t", k=KD)
        qT = cut(H * T).rearrange("p (h t) -> p h t", h=H)
        v = cut(NT * BW).rearrange("p (t e) -> p t e", t=NT)
        cumG, dref, expn, dlast = ([cut(T) for _ in range(2)] for _ in range(4))
        kdn = [cut(NT * 2 * P).rearrange("p (j i d) -> p j i d", j=NT, i=2) for _ in range(2)]
        PT = [cut(NT * P) for _ in range(2)]
        state = [cut(NCH * P).rearrange("p (n e) -> p n e", n=NCH) for _ in range(2)]
        decay = [cut(NCH) for _ in range(2)]
        hcst = cut(S_N)
        at[0] = 0
        ring = cut(RING * 2 * D).rearrange("p (s n) -> p s n", s=RING)
        h2 = cut(NT * D).rearrange("p (t n) -> p t n", t=NT)
        x2 = cut(TPH * D).rearrange("p (t n) -> p t n", t=TPH)
        tv, tif = (cut(HP * TOP).rearrange("p (s k) -> p s k", s=HP) for _ in range(2))
        ti = cut(HP * TOP).bitcast(U32).rearrange("p (s k) -> p s k", s=HP)
        cs, ci = (cut(PH * NCAND).rearrange("p (h c) -> p h c", h=PH) for _ in range(2))
        bs, posf = (cut(SLOTS).rearrange("p (h k) -> p h k", h=PH) for _ in range(2))
        pos = cut(SLOTS).bitcast(U32).rearrange("p (h k) -> p h k", h=PH)
        eq = cut(TOP * NCAND).rearrange("p (k c) -> p k c", k=TOP)
        gate = cut(NT * SLOTS).rearrange("p (t s) -> p t s", t=NT)
        idx = cut(NT * SLOTS).bitcast(U32).rearrange("p (t s) -> p t s", t=NT)
        x2_dram = nc.dram_tensor("x2_kept", (T, D), F32, kind="Internal").ap()

        banks = [ctx.enter_context(nc.psum_tensor(f"bank{i}", [P, 512], F32)) for i in range(6)]
        wide = ctx.enter_context(nc.psum_tensor("wide", [P, 1024], F32))
        bankA, bankB = banks[0:2], banks[2:4]
        tp, scb = banks[4], banks[5]

        x_in, c_in, mem_in, late_in = sem("x_in"), sem("c_in"), sem("mem_in"), sem("late_in")
        w_in = [sem(f"w_in{i}") for i in range(WSLOTS)]
        A_full, A_free = sem("A_full"), sem("A_free")
        B_full, B_free = sem("B_full"), sem("B_free")
        v_ord, a_ord = sem("v_ord"), sem("a_ord")
        sq_done, root, eps_done, lb_exp = sem("sq_done"), sem("root"), sem("eps_done"), sem("lb_exp")
        h_done, m_done = sem("h_done"), sem("m_done")
        lb_done = sem("lb_done")
        zero_done = sem("zero_done")
        logf_done = sem("logf_done")
        dsub, exps, prods = sem("dsub"), sem("exps"), sem("prods")
        kd_turned, kd_copied = sem("kd_turned"), sem("kd_copied")
        sc_made, sc_masked = sem("sc_made"), sem("sc_masked")
        ds_made, st_done = sem("ds_made"), sem("st_done")
        o_made, o_kept = sem("o_made"), sem("o_kept")
        y1_done = sem("y1_done")
        lg_made, mx_done, pexp, pnorm = sem("lg_made"), sem("mx_done"), sem("pexp"), sem("pnorm")
        p_turned, pT_done, pv_made, y2_done = sem("p_turned"), sem("pT_done"), sem("pv_made"), sem("y2_done")
        osq_done, y0_done = sem("osq_done"), sem("y0_done")
        x_nat, x2_kept = sem("x_nat"), sem("x2_kept")
        ssq_done, h2_done = sem("ssq_done"), sem("h2_done")
        gd_done, ge_done, idx_done, gate_done = sem("gd_done"), sem("ge_done"), sem("idx_done"), sem("gate_done")
        landed = [sem(f"landed{i}") for i in range(RING)]
        staged, seen = sem("staged"), sem("seen")
        dot, gel, wgt, dia, used = sem("dot"), sem("gel"), sem("wgt"), sem("dia"), sem("used")
        back_in, drained, fsq, fdone, out_done = sem("back_in"), sem("drained"), sem("fsq"), sem("fdone"), sem("out_done")
        top1_done, lb_diff = sem("top1_done"), sem("lb_diff")
        last_before_hg = {}
        for f in range(HALVES):
            before = steps[:steps.index(("hg", f, 0))]
            last_before_hg[f] = [key for s in before for r, key in chunks_of(s) if r == "B"][-1]

        full = {"A": A_full, "B": B_full}
        free = {"A": A_free, "B": B_free}

        def n_of(r, key):
            return place[r][key] + 1

        def bank_of(r, key):
            return (bankA if r == "A" else bankB)[place[r][key] % 2]

        def wblock(step, i):
            b = block_of[step, i]
            kc = blocks[b][1][2] // P
            return W[:, b % WSLOTS, 0:kc * WCOLS].rearrange("p (k n) -> p k n", k=kc)

        def window(f):
            return (0, 0 + HALF + 1, 1) if f == 0 else (HALF - 1, HALF + 1, 0)

        src = {"in": a["w_in"], "kv": a["w_kv"], "br": a["w_br"], "out": a["w_out"], "pq": a["w_pq"]}
        xn = a["x"].rearrange("(t p) n -> t p n", p=P)
        outn = out.rearrange("b (t p) n -> (b t) p n", p=P)
        x2n = x2_dram.rearrange("(t p) n -> t p n", p=P)

        def land_count(g):
            return 16 * (g // RING + 1)

        block = ctx.enter_context(nc.Block())

        @block.sync
        def _(sp):
            sp.dma_start(memT, a["memT"].rearrange("(k p) t -> p k t", p=P)).then_inc(mem_in, 16)
            sp.dma_start(cst[:, :], a["cst"]).then_inc(c_in, 16)
            sp.dma_start(vec[:, :], a["vec"]).then_inc(c_in, 16)
            xT_v = a["xT"].rearrange("(k p) t -> p k t", p=P)
            for i in range(4):
                sp.dma_start(hT[:, 2 * i:2 * i + 2, :], xT_v[:, 2 * i:2 * i + 2, :]).then_inc(x_in, 16)
            sp.dma_start(hcst, a["hcst"]).then_inc(c_in, 16)
            spill_at = {b: s[1] for b, (s, _) in enumerate(blocks) if s[0] == "pq" and s[2] == 5}
            xload_at = {b: s[1] for b, (s, _) in enumerate(blocks) if s[0] == "wout" and s[2] == 0}
            for b, (s, (name, r0, rows, c0, cols)) in enumerate(blocks):
                if b >= WSLOTS:
                    r, key = last_piece[blocks[b - WSLOTS][0]]
                    sp.wait_ge(full[r], n_of(r, key))
                kc = rows // P
                sp.dma_start(W[:, b % WSLOTS, 0:kc * cols].rearrange("p (k n) -> p k n", k=kc),
                             src[name][r0:r0 + rows, c0:c0 + cols].rearrange("(k p) n -> p k n", p=P))\
                  .then_inc(w_in[b % WSLOTS], 16)
                if b == 5:
                    sp.dma_start(keys[:, :], a["keys"]).then_inc(late_in, 16)
                    sp.dma_start(g_ffn[:, :], a["g_ffn"]).then_inc(late_in, 16)
                    sp.dma_start(g_fin[:, :], a["g_fin"]).then_inc(late_in, 16)
                if b in xload_at:
                    f = xload_at[b]
                    if f == 0:
                        sp.wait_ge(o_kept, H)
                    else:
                        sp.wait_ge(x2_kept, 16 * TPH * f)
                        sp.wait_ge(h2_done, TPH * f)
                    for t in range(TPH):
                        sp.dma_start(x2[:, t, :], xn[TPH * f + t]).then_inc(x_nat, 16)
                if b in spill_at:
                    f = spill_at[b]
                    sp.wait_ge(B_free, n_of("B", ("wout", f, 3, TPH - 1)))
                    for t in range(TPH):
                        sp.dma_start(x2n[TPH * f + t], x2[:, t, :]).then_inc(x2_kept, 16)
            sp.wait_ge(x2_kept, 16 * NT)
            sp.wait_ge(out_done, 16 * NT)

        @block.gpsimd
        def _(pool):
            def issue(t, k, s, it):
                g = t * SLOTS + k
                pool.wait_ge(used, it * RING + (g + 1))
                col = idx[:, t, bass.ds(it * RING + k, 1)] if not isinstance(it, int) else idx[:, t, k:k + 1]
                nc.gpsimd.tensor_copy(stage[:, s, :], col).then_inc(staged, 1)
                pool.wait_ge(staged, it * RING + (g + 1))
                pool.sem_inc(seen, 1)
                pool.indirect_dma_start(ring[:, s, :], None, a["uv"],
                                        bass.IndirectOffsetOnAxis(ap=stage[:, s, :], axis=0)).then_inc(landed[s], 16)

            n = SLOTS // QH
            for t in range(NT):
                for g in range(QH):
                    pool.wait_ge(idx_done, QH * t + g + 1)
                    k = n * g
                    with pool.Fori(0, n // RING) as it:
                        for i in range(RING):
                            issue(t, k + i, (t * SLOTS + k + i) % RING, it)
                    for i in range(n // RING * RING, n):
                        issue(t, k + i, (t * SLOTS + k + i) % RING, 0)

        @block.tensor
        def _(pe):
            mm = nc.tensor.matmul

            def open_piece(r, key):
                n = n_of(r, key)
                if n > 2:
                    pe.wait_ge(free[r], n - 2)
                return bank_of(r, key)

            def need_weights(step, i):
                b = block_of[step, i]
                pe.wait_ge(w_in[b % WSLOTS], 16 * (b // WSLOTS + 1))
                return wblock(step, i)

            def project(r, key, outp, lhs, rhs, kc=KD):
                for k in range(kc):
                    last = mm(outp, lhs(k), rhs(k), start=(k == 0), stop=(k == kc - 1))
                last.then_inc(full[r], 1)

            def products(t, k, s, it):
                g = t * SLOTS + k
                pe.wait_ge(dia, it * RING + (g + 1))
                for c in range(2):
                    last = mm(wide[:, 512 * c:512 * c + 512], diag[:, s, :], ring[:, s, D + 512 * c:D + 512 * c + 512],
                              start=False, stop=False, skip_group_check=True)
                last.then_inc(used, 1)

            for step in tensor_order(steps):
                kind = step[0]
                pieces = chunks_of(step)
                if kind in ("norm_in", "norm_mem"):
                    bank = open_piece(*pieces[0])
                    sq, n, c0 = (sqx, T, KD) if kind == "norm_in" else (sqm, NMEM, 0)
                    pe.wait_ge(c_in, 48)
                    for k in range(KD):
                        pe.wait_ge(sq_done, c0 + k + 1)
                        last = mm(bank[:, 0:n], ones, sq[:, k, :], start=(k == 0), stop=(k == KD - 1))
                    last.then_inc(A_full, 1)
                elif kind == "kv":
                    b = step[1]
                    w = need_weights(step, 0)
                    pe.wait_ge(m_done, KD)
                    for c in range(2):
                        r, key = pieces[c]
                        bank = open_piece(r, key)
                        if b < 2:
                            project(r, key, bank[:, 0:NMEM], lambda k: w[:, k, c * P:c * P + P], lambda k: memT[:, k, :])
                        else:
                            project(r, key, bank[:, 0:WCOLS], lambda k: memT[:, k, c * P:c * P + P], lambda k: w[:, k, :])
                elif kind in ("z", "q"):
                    w = need_weights(step, 0)
                    pe.wait_ge(h_done, KD)
                    for c in range(2):
                        r, key = pieces[c]
                        bank = open_piece(r, key)
                        project(r, key, bank[:, :], lambda k: w[:, k, c * P:c * P + P], lambda k: hT[:, k, :])
                elif kind == "v":
                    w = need_weights(step, 0)
                    for t in range(NT):
                        r, key = pieces[t]
                        bank = open_piece(r, key)
                        project(r, key, bank[:, 0:WCOLS], lambda k: hT[:, k, t * P:t * P + P], lambda k: w[:, k, :])
                elif kind == "conv":
                    _, f, b, c = step
                    t0, n, _ = window(f)
                    for i, (r, key) in enumerate(pieces):
                        w = need_weights((*step[:3], 0), i)
                        bank = open_piece(r, key)
                        t1, m = (t0, n) if i < 2 else (f * HALF, HALF)
                        project(r, key, bank[:, 0:m], lambda k: w[:, k, c * P:c * P + P], lambda k: hT[:, k, t1:t1 + m])
                elif kind == "mq":
                    w = need_weights(step, 0)
                    f = step[1]
                    for c in range(2):
                        r, key = pieces[c]
                        bank = open_piece(r, key)
                        project(r, key, bank[:, 0:HALF], lambda k: w[:, k, c * P:c * P + P],
                                lambda k: hT[:, k, f * HALF:(f + 1) * HALF])
                elif kind == "branch":
                    _, f, n, b = step
                    wg, wb = need_weights(step, 0), need_weights(step, 1)
                    done = {1: (y1_done, BC), 2: (y2_done, H), 0: (y0_done, H)}[n]
                    for c in range(2):
                        r, key = pieces[2 * c]
                        bank = open_piece(r, key)
                        project(r, key, bank[:, 0:HALF], lambda k: wg[:, k, c * P:c * P + P],
                                lambda k: hT[:, k, f * HALF:(f + 1) * HALF])
                        r, key = pieces[2 * c + 1]
                        bank = open_piece(r, key)
                        pe.wait_ge(done[0], done[1] * (f + 1))
                        project(r, key, bank[:, 0:HALF], lambda k: wb[:, k, c * P:c * P + P],
                                lambda k: y[n][:, k, :], BC)
                elif kind == "hg":
                    _, f, b = step
                    w = need_weights(step, 0)
                    for c in range(2):
                        h = 2 * b + c
                        r, key = pieces[2 * c]
                        bank = open_piece(r, key)
                        project(r, key, bank[:, 0:HALF], lambda k: w[:, k, c * P:c * P + P],
                                lambda k: hT[:, k, f * HALF:(f + 1) * HALF])
                        r, key = pieces[2 * c + 1]
                        bank = open_piece(r, key)
                        pe.wait_ge(osq_done, f * H + h + 1)
                        mm(bank[:, 0:HALF], ones, tmp[:, c, :], start=True, stop=True).then_inc(A_full, 1)
                elif kind == "intra":
                    _, h, d = step
                    u = 2 * h + d
                    pe.wait_ge(prods, 4 * u + 4)
                    if u >= 1:
                        pe.wait_ge(kd_copied, u)
                    if d == 0 and h >= 1:
                        pe.wait_ge(o_kept, h)
                    for j in range(NT):
                        last = nc.tensor.transpose(tp[:, j * P:j * P + P], dlast[d][:, j * P:j * P + P], ident)
                    last.then_inc(kd_turned, 1)
                    if u >= 1:
                        pe.wait_ge(sc_masked, u)
                    for j in range(NT):
                        cols = slice(j * P, j * P + P)
                        last = mm(scb[:, cols], expn[d][:, cols], dref[d][:, cols], start=True, stop=True)
                    last.then_inc(sc_made, 1)
                    pe.wait_ge(kd_copied, u + 1)
                    if u >= 1:
                        pe.wait_ge(st_done, u)
                    for n in range(NCH):
                        last = mm(wide[:, n * P:n * P + P], kdn[d][:, n // 2, n % 2, :],
                                  v[:, n // 2, h * P:h * P + P], start=True, stop=True)
                    last.then_inc(ds_made, 1)
                elif kind == "o":
                    h = step[1]
                    pe.wait_ge(sc_masked, 2 * h + 2)
                    pe.wait_ge(st_done, 2 * h + 2)
                    for j in range(NT):
                        cols = slice(j * P, j * P + P)
                        vj = v[:, j, h * P:h * P + P]
                        mm(tp[:, cols], vj, PT[0][:, cols], start=True, stop=False, skip_group_check=True)
                        last = mm(tp[:, cols], vj, PT[1][:, cols], start=False, stop=False, skip_group_check=True)
                        work = [(d, n) for n in (2 * j, 2 * j + 1) for d in range(2)
                                if not (d == 0 and n == 0) and not (d == 1 and n == NCH - 1)]
                        for d, n in work:
                            cc = slice(n * CH, n * CH + CH)
                            last = mm(tp[:, cc], state[d][:, n, :], cumG[d][:, cc], start=False,
                                      stop=(d, n) == work[-1], skip_group_check=True)
                    last.then_inc(o_made, 1)
                elif kind == "att":
                    _, f, h = step
                    u = H * f + h
                    r_mq = ("A", ("mq", f, h // 2, h % 2))
                    pe.wait_ge(A_free, n_of(*r_mq))
                    if u >= 1:
                        pe.wait_ge(pexp, TPH * u)
                    else:
                        pe.wait_ge(sc_masked, 2 * H)
                        pe.wait_ge(o_kept, H)
                    for t in range(TPH):
                        last = mm(scb[:, t * NMEM:(t + 1) * NMEM], mqT[:, h, t * P:t * P + P], mkT[:, h, :],
                                  start=True, stop=True)
                    last.then_inc(lg_made, 1)
                    if u >= 1:
                        pe.wait_ge(y2_done, u)
                    pe.wait_ge(pnorm, u + 1)
                    for m in range(2):
                        for t in range(TPH):
                            last = nc.tensor.transpose(tp[:, m * HALF + t * P:m * HALF + t * P + P],
                                                       prob[:, t, m * P:m * P + P], ident)
                    last.then_inc(p_turned, 1)
                    pe.wait_ge(pT_done, u + 1)
                    for m in range(2):
                        last = mm(tp[:, 0:HALF], mv[:, m, h * P:h * P + P], probT[:, m, :], start=(m == 0), stop=(m == 1))
                    last.then_inc(pv_made, 1)
                elif kind == "wout":
                    _, f, b = step
                    w = need_weights(step, 0)
                    pe.wait_ge(B_free, n_of("B", ("branch", f, BRANCH_ORDER[-1], 3, "br", 1)))
                    for t in range(TPH):
                        r, key = pieces[t]
                        bank = open_piece(r, key)
                        project(r, key, bank[:, 0:WCOLS], lambda k: merged[:, k, t * P:t * P + P], lambda k: w[:, k, :])
                elif kind == "turn":
                    f = step[1]
                    for i, (r, key) in enumerate(pieces):
                        t, g = i // 2, i % 2
                        bank = open_piece(r, key)
                        pe.wait_ge(h2_done, TPH * f + t + 1)
                        for k in range(4):
                            last = nc.tensor.transpose(bank[:, k * P:k * P + P],
                                                       h2[:, TPH * f + t, (4 * g + k) * P:(4 * g + k + 1) * P], ident)
                        last.then_inc(A_full, 1)
                elif kind == "pq":
                    _, f, b = step
                    w = need_weights(step, 0)
                    pe.wait_ge(A_free, n_of("A", ("turn", f, TPH - 1, 1)))
                    pe.wait_ge(late_in, 48)
                    for c in range(2):
                        r, key = pieces[c]
                        bank = open_piece(r, key)
                        project(r, key, bank[:, 0:HALF], lambda k: w[:, k, c * P:c * P + P], lambda k: merged[:, k, :])
                    for c in range(2):
                        hp = 2 * b + c
                        r, key = pieces[2 + c]
                        bank = open_piece(r, key)
                        pe.wait_ge(A_free, n_of(*pieces[c]))
                        for t in range(TPH):
                            last = mm(bank[:, t * P:t * P + P], qpT[:, c, t * P:t * P + P], keys[:, hp * NK:hp * NK + NK],
                                      start=True, stop=True)
                        last.then_inc(A_full, 1)
                elif kind == "open":
                    t = step[1]
                    if t == 0:
                        pe.wait_ge(st_done, 2 * H)
                        pe.sem_inc(used, RING)
                    else:
                        pe.wait_ge(drained, t)
                    for c in range(2):
                        mm(wide[:, 512 * c:512 * c + 512], zeros, keys[:, 0:512], start=True, stop=False,
                           skip_group_check=True)
                elif kind == "gather":
                    _, t, k, n = step
                    whole = n // RING
                    if whole > 1:
                        with pe.Fori(0, whole) as it:
                            for s in range(RING):
                                products(t, k + s, (t * SLOTS + k + s) % RING, it)
                    else:
                        whole = 0
                    for i in range(whole * RING, n):
                        products(t, k + i, (t * SLOTS + k + i) % RING, 0)

        @block.scalar
        def _(act):
            done = [0]
            af = nc.scalar.activation

            def then_wait(ins):
                done[0] += 1
                ins.then_inc(a_ord, 1)
                act.wait_ge(a_ord, done[0])

            def turn_in(r, key):
                act.wait_ge(full[r], n_of(r, key))
                return bank_of(r, key)

            def gather_body(t, k, n, it):
                g = t * SLOTS + k
                for c in range(0, n, GROUP):
                    m = min(GROUP, n - c)
                    act.wait_ge(dot, it * RING + (g + c + m))
                    s = (g + c) % RING
                    af(acts[:, 1, s:s + m], acts[:, 0, s:s + m], ACT.Gelu).then_inc(gel, 1)
                    act.wait_ge(gel, it * (RING // GROUP) + (g + c) // GROUP + 1)
                    for i in range(c, c + m):
                        s = (g + i) % RING
                        col = gate[:, t, k + i:k + i + 1] if isinstance(it, int) else gate[:, t, bass.ds(it * RING + (k + i), 1)]
                        af(acts[:, 2, s:s + 1], acts[:, 1, s:s + 1], ACT.Copy, scale=col).then_inc(wgt, 1)
                    act.wait_ge(wgt, it * RING + (g + c + m))
                    for i in range(c, c + m):
                        s = (g + i) % RING
                        af(diag[:, s, :], ident, ACT.Copy, scale=acts[:, 2, s:s + 1]).then_inc(dia, 1)

            for step in steps:
                kind = step[0]
                pieces = chunks_of(step)
                if kind in ("norm_in", "norm_mem"):
                    raw, sq, n, there, done_, full_in = (hT, sqx, T, h_done, 64, x_in) if kind == "norm_in" else \
                        (memT, sqm, NMEM, m_done, 16, mem_in)
                    act.wait_ge(full_in, done_)
                    for k in range(KD):
                        af(sq[:, k, :], raw[:, k, :], ACT.Square).then_inc(sq_done, 1)
                    act.wait_ge(eps_done, 1)
                    bank = turn_in(*pieces[0])
                    af(bank[:, 0:n], bank[:, 0:n], ACT.Sqrt, scale=1.0 / D, bias=eps[:, :]).then_inc(root, 1)
                    act.wait_ge(there, KD)
                    act.sem_inc(A_free, 1)
                    if kind == "norm_in":
                        act.wait_ge(lb_diff, 2)
                        af(lbs[:, 0:2, :], lbs[:, 0:2, :], ACT.Exp).then_inc(lb_exp, 1)
                elif kind == "kv":
                    for c in range(2):
                        bank = turn_in(*pieces[c])
                        b = step[1]
                        dst = mkT[:, 2 * b + c, :] if b < 2 else mv[:, c, (b - 2) * WCOLS:(b - 1) * WCOLS]
                        af(dst, bank[:, 0:NMEM], ACT.Copy).then_inc(A_free, 1)
                elif kind == "z":
                    _, d, b = step
                    for c in range(2):
                        h = 2 * b + c
                        bank = turn_in(*pieces[c])
                        af(sig[:, d, h, :], bank[:, :], ACT.Sigmoid)
                        af(sgn[:, d, h, :], bank[:, :], ACT.Sigmoid, scale=-1.0).then_inc(A_free, 1)
                elif kind == "q":
                    for c in range(2):
                        bank = turn_in(*pieces[c])
                        af(qT[:, 2 * step[1] + c, :], bank[:, :], ACT.Silu).then_inc(A_free, 1)
                elif kind == "v":
                    for t in range(NT):
                        bank = turn_in(*pieces[t])
                        af(v[:, t, step[1] * WCOLS:(step[1] + 1) * WCOLS], bank[:, 0:WCOLS], ACT.Copy).then_inc(A_free, 1)
                elif kind == "logf":
                    act.wait_ge(lb_done, 1)
                    act.wait_ge(A_free, n_of("A", ("z", 1, 1, 1)))
                    for h in range(H):
                        for d in range(2):
                            u = 4 * d + h
                            af(sig[:, d, h, :], sig[:, d, h, :], ACT.Ln, scale=lbs[:, 1, u:u + 1],
                               bias=lbs[:, 0, u:u + 1]).then_inc(logf_done, 1)
                elif kind == "elem":
                    _, h, d = step
                    u = 2 * h + d
                    act.wait_ge(dsub, 2 * u + 2)
                    af(expn[d][:, :], dref[d][:, :], ACT.Exp, scale=-1.0).then_inc(exps, 1)
                    af(dlast[d][:, :], dlast[d][:, :], ACT.Exp).then_inc(exps, 1)
                    af(cumG[d][:, :], cumG[d][:, :], ACT.Exp).then_inc(exps, 1)
                    act.wait_ge(exps, 4 * u + 1)
                    af(dref[d][:, :], dref[d][:, :], ACT.Exp).then_inc(exps, 1)
                elif kind == "intra":
                    _, h, d = step
                    u = 2 * h + d
                    act.wait_ge(kd_turned, u + 1)
                    act.wait_ge(zero_done, 2)
                    for i in range(2):
                        rows = slice(CH * i, CH * i + CH)
                        last = af(kdn[d][rows, :, i, :], tp[rows, :].rearrange("p (j e) -> p j e", j=NT), ACT.Copy)
                    last.then_inc(kd_copied, 1)
                elif kind == "o":
                    h = step[1]
                    act.wait_ge(o_made, h + 1)
                    af(oT[:, h, :], tp[:, :], ACT.Copy).then_inc(o_kept, 1)
                elif kind == "conv":
                    _, f, b, c = step
                    n = window(f)[1]
                    bank = turn_in(*pieces[0])
                    g = (f * 2 + b) * 2 + c
                    if f:
                        act.wait_ge(y0_done, H * f)
                    if g >= 2:
                        act.wait_ge(y1_done, g - 1)
                    af(csb[:, c, 0:n], bank[:, 0:n], ACT.Copy).then_inc(A_free, 1)
                elif kind == "mq":
                    for c in range(2):
                        bank = turn_in(*pieces[c])
                        if step[1] >= 1:
                            act.wait_ge(top1_done, QH * TPH * step[1])
                        af(mqT[:, 2 * step[2] + c, :], bank[:, 0:HALF], ACT.Copy).then_inc(A_free, 1)
                elif kind == "att":
                    _, f, h = step
                    u = H * f + h
                    act.wait_ge(mx_done, u + 1)
                    if u >= 1:
                        act.wait_ge(p_turned, u)
                    for t in range(TPH):
                        af(prob[:, t, :], scb[:, t * NMEM:(t + 1) * NMEM], ACT.Exp, scale=float(P) ** -0.5,
                           bias=tiny[:, t:t + 1], accum_out=tiny[:, 4 + t:5 + t]).then_inc(pexp, 1)
                    act.wait_ge(p_turned, u + 1)
                    if u >= 1:
                        act.wait_ge(pv_made, u)
                    af(probT, tp[:, :].rearrange("p (m t) -> p m t", m=2), ACT.Copy).then_inc(pT_done, 1)
                    act.wait_ge(pv_made, u + 1)
                    af(y[2][:, h, :], tp[:, 0:HALF], ACT.Copy).then_inc(y2_done, 1)
                elif kind == "branch":
                    _, f, n, b = step
                    for c in range(2):
                        r, key = pieces[2 * c]
                        bank = turn_in(r, key)
                        before = [k for k in order["B"][:place["B"][pieces[2 * c + 1][1]]] if k[0] == "branch"][-2:]
                        if len(before) == 2:
                            act.wait_ge(B_free, n_of("B", before[0]))
                        if n == 0:
                            act.wait_ge(y0_done, H * (f + 1))
                        af(gsb[:, c, :], bank[:, 0:HALF], ACT.Sigmoid).then_inc(A_free, 1)
                elif kind == "hg":
                    _, f, b = step
                    if f or b:
                        act.wait_ge(y0_done, f * H + 2 * b)
                    for c in range(2):
                        h = 2 * b + c
                        act.wait_ge(o_kept, H)
                        act.wait_ge(B_free, n_of("B", last_before_hg[f]))
                        af(tmp[:, c, :], oT[:, h, f * HALF:(f + 1) * HALF], ACT.Square).then_inc(osq_done, 1)
                    for c in range(2):
                        bank = turn_in(*pieces[2 * c])
                        af(csb[:, c, 0:HALF], bank[:, 0:HALF], ACT.Silu).then_inc(A_free, 1)
                        bank = turn_in(*pieces[2 * c + 1])
                        af(gsb[:, c, :], bank[:, 0:HALF], ACT.Sqrt, scale=1.0 / P, bias=eps[:, :]).then_inc(A_free, 1)
                elif kind == "ffn":
                    f = step[1]
                    for t in range(TPH):
                        act.wait_ge(B_free, n_of("B", ("wout", f, 3, TPH - 1)))
                        then_wait(af(junk[:, :], x2[:, t, :], ACT.Square, accum_out=tiny[:, 8 + t:9 + t]))
                        af(tiny[:, 10 + t:11 + t], tiny[:, 8 + t:9 + t], ACT.Sqrt, scale=1.0 / D,
                           bias=eps[:, :]).then_inc(ssq_done, 1)
                elif kind == "turn":
                    f = step[1]
                    for i, (r, key) in enumerate(pieces):
                        t, g = i // 2, i % 2
                        bank = turn_in(r, key)
                        af(merged[:, 4 * g:4 * g + 4, t * P:t * P + P], bank[:, :].rearrange("p (k t) -> p k t", k=4),
                           ACT.Copy).then_inc(A_free, 1)
                elif kind == "pq":
                    _, f, b = step
                    for c in range(2):
                        bank = turn_in(*pieces[c])
                        if b or f:
                            prev = ("pq", f, b - 1, "s", c) if b else ("pq", f - 1, HP // 2 - 1, "s", c)
                            act.wait_ge(A_full, n_of("A", prev))
                        af(qpT[:, c, :], bank[:, 0:HALF], ACT.Copy).then_inc(A_free, 1)
                    for c in range(2):
                        hp = 2 * b + c
                        bank = turn_in(*pieces[2 + c])
                        af(score[:, :, hp * NK:hp * NK + NK], bank[:, 0:TPH * P].rearrange("p (t k) -> p t k", t=TPH),
                           ACT.Copy).then_inc(A_free, 1)
                elif kind == "look":
                    _, t, g = step
                    bq = bs[:, HQ * g:HQ * (g + 1), :]
                    act.wait_ge(gd_done, QH * t + g + 1)
                    af(bq, bq, ACT.Exp).then_inc(ge_done, 1)
                elif kind == "gather":
                    _, t, k, n = step
                    act.wait_ge(gate_done, QH * t + (k + n - 1) // (SLOTS // QH) + 1)
                    whole = n // RING
                    if whole > 1:
                        with act.Fori(0, whole) as it:
                            gather_body(t, k, RING, it)
                    else:
                        whole = 0
                    if n > whole * RING:
                        gather_body(t, k + whole * RING, n - whole * RING, 0)
                elif kind == "drain":
                    t = step[1]
                    act.wait_ge(x2_kept, 16 * TPH * (t // TPH + 1))
                    act.wait_ge(dot, (t + 1) * SLOTS)
                    act.dma_start(h2[:, t, :], x2n[t]).then_inc(back_in, 16)
                elif kind == "last":
                    t = step[1]
                    act.wait_ge(drained, t + 1)
                    then_wait(af(junk[:, :], h2[:, t, :], ACT.Square, accum_out=tiny[:, 16:17]))
                    af(tiny[:, 17:18], tiny[:, 16:17], ACT.Sqrt, scale=1.0 / D, bias=eps[:, :]).then_inc(fsq, 1)
                    act.wait_ge(fdone, t + 1)
                    act.dma_start(outn[t], h2[:, t, :]).then_inc(out_done, 16)
            act.wait_ge(out_done, 16 * NT)

        @block.vector
        def _(dve):
            done = [0]
            ve = nc.vector

            def tick(ins):
                done[0] += 1
                ins.then_inc(v_ord, 1)

            def settle():
                dve.wait_ge(v_ord, done[0])

            def link(ins):
                tick(ins)
                settle()

            def turn_in(r, key):
                dve.wait_ge(full[r], n_of(r, key))
                return bank_of(r, key)

            def dots(t, k, n, it):
                for i in range(n):
                    g = t * SLOTS + k + i
                    s = g % RING
                    dve.wait_ge(landed[s], it * 16 + land_count(g))
                    ve.tensor_tensor_reduce(ring[:, s, 0:D], ring[:, s, 0:D], h2[:, t, :], 1.0, 0.0, ALU.mult, ALU.add,
                                            acts[:, 0, s:s + 1]).then_inc(dot, 1)

            for step in steps:
                kind = step[0]
                pieces = chunks_of(step)
                if kind == "norm_mem":
                    dve.wait_ge(c_in, 48)
                    l0, l1 = vec[:, V_LB:V_LB + 8], vec[:, V_LB + 8:V_LB + 16]
                    ve.memset(eps[:, :], EPS).then_inc(eps_done, 1)
                    link(ve.tensor_tensor(lbs[:, 2, :], l0, l1, ALU.max))
                    ve.tensor_tensor(lbs[:, 0, :], l0, lbs[:, 2, :], ALU.subtract).then_inc(lb_diff, 1)
                    ve.tensor_tensor(lbs[:, 1, :], l1, lbs[:, 2, :], ALU.subtract).then_inc(lb_diff, 1)
                if kind in ("norm_in", "norm_mem"):
                    src_t, n, g0, dn = (hT, T, V_MIX, h_done) if kind == "norm_in" else (memT, NMEM, V_MEM, m_done)
                    r, key = pieces[0]
                    bank = turn_in(r, key)
                    dve.wait_ge(root, n_of(r, key))
                    link(ve.reciprocal(bank[:, 0:n], bank[:, 0:n]))
                    for k in range(KD):
                        last = ve.scalar_tensor_tensor(out=src_t[:, k, :], in0=src_t[:, k, :], scalar=vec[:, g0 + k:g0 + k + 1],
                                                       in1=bank[:, 0:n], op0=ALU.mult, op1=ALU.mult)
                        last.then_inc(dn, 1)
                elif kind == "kv" and step[1] == 0:
                    dve.wait_ge(lb_exp, 1)
                    link(ve.tensor_tensor(lbs[:, 2, :], lbs[:, 0, :], lbs[:, 1, :], ALU.add))
                    link(ve.reciprocal(lbs[:, 2, :], lbs[:, 2, :]))
                    link(ve.tensor_tensor(lbs[:, 0, :], lbs[:, 0, :], lbs[:, 2, :], ALU.mult))
                    ve.tensor_scalar(lbs[:, 1, :], lbs[:, 0, :], -1.0, 1.0, ALU.mult, ALU.add).then_inc(lb_done, 1)
                    for d in range(2):
                        tick(ve.memset(PT[d][:, :], 0.0))
                    for d in range(2):
                        ve.memset(kdn[d][:, :, :, :], 0.0).then_inc(zero_done, 1)
                    ve.memset(ub[:, :, :], 0.0).then_inc(zero_done, 1)
                elif kind == "elem":
                    _, h, d = step
                    u = 2 * h + d
                    dve.wait_ge(logf_done, u + 1)
                    dve.wait_ge(A_free, n_of("A", ("q", 1, 1)))
                    if h >= 1:
                        dve.wait_ge(o_made, h)
                    lf = sig[:, d, h, :]
                    G = cumG[d]
                    if d == 0:
                        link(ve.tensor_tensor_scan(G[:, :], hcst[:, S_KEEP:S_KEEP + T], lf, 0.0, ALU.mult, ALU.add))
                    else:
                        link(ve.tensor_tensor_scan(G[:, ::-1], hcst[:, S_KEEP:S_KEEP + T], lf[:, ::-1], 0.0, ALU.mult, ALU.add))
                    mid, end = (CH // 2 - 1, CH - 1) if d == 0 else (CH // 2, 0)
                    Gc = G[:, :].rearrange("p (n c) -> p n c", c=CH)
                    ve.tensor_tensor(dref[d][:, :].rearrange("p (n c) -> p n c", c=CH), Gc,
                                     Gc[:, :, mid:mid + 1].to_broadcast([P, NCH, CH]), ALU.subtract).then_inc(dsub, 1)
                    ve.tensor_tensor(dlast[d][:, :].rearrange("p (n c) -> p n c", c=CH),
                                     Gc[:, :, end:end + 1].to_broadcast([P, NCH, CH]), Gc, ALU.subtract).then_inc(dsub, 1)
                    lb1 = lbs[:, 1, 4 * d + h:4 * d + h + 1]
                    k_ = sgn[:, d, h, :]
                    dve.wait_ge(exps, 4 * u + 1)
                    ve.scalar_tensor_tensor(out=expn[d][:, :], in0=k_, scalar=lb1, in1=expn[d][:, :],
                                            op0=ALU.mult, op1=ALU.mult).then_inc(prods, 1)
                    dve.wait_ge(exps, 4 * u + 2)
                    ve.scalar_tensor_tensor(out=dlast[d][:, :], in0=k_, scalar=lb1, in1=dlast[d][:, :],
                                            op0=ALU.mult, op1=ALU.mult).then_inc(prods, 1)
                    dve.wait_ge(exps, 4 * u + 4)
                    tick(ve.tensor_copy(decay[d][:, :], Gc[:, :, end]))
                    ve.tensor_tensor(dref[d][:, :], dref[d][:, :], qT[:, h, :], ALU.mult).then_inc(prods, 1)
                    settle()
                    ve.tensor_tensor(G[:, :], G[:, :], qT[:, h, :], ALU.mult).then_inc(prods, 1)
                elif kind == "intra":
                    _, h, d = step
                    u = 2 * h + d
                    dve.wait_ge(sc_made, u + 1)
                    settle()
                    m = hcst[:, (S_MF, S_MB)[d]:(S_MF, S_MB)[d] + P].bitcast(U32)
                    ve.copy_predicated(PT[d][:, :].rearrange("p (j t) -> p j t", j=NT),
                                       m.unsqueeze(1).to_broadcast([P, NT, P]),
                                       scb[:, :].rearrange("p (j t) -> p j t", j=NT)).then_inc(sc_masked, 1)
                    dve.wait_ge(ds_made, u + 1)
                    seq = list(range(NCH)) if d == 0 else list(range(NCH - 1, -1, -1))
                    st = state[d]
                    for i in range(NCH - 1):
                        n, nx = seq[i], seq[i + 1]
                        dS = wide[:, n * P:n * P + P]
                        if i == 0:
                            ins = ve.tensor_copy(st[:, nx, :], dS)
                        else:
                            ins = ve.scalar_tensor_tensor(out=st[:, nx, :], in0=st[:, n, :], scalar=decay[d][:, n:n + 1],
                                                          in1=dS, op0=ALU.mult, op1=ALU.add)
                        if i < NCH - 2:
                            link(ins)
                        else:
                            ins.then_inc(st_done, 1)
                elif kind == "conv":
                    _, f, b, c = step
                    t0, n, c0 = window(f)
                    ch = 2 * b + c
                    bank = turn_in(*pieces[1])
                    dve.wait_ge(A_free, n_of(*pieces[0]))
                    dve.wait_ge(zero_done, 3)
                    if f == 1 and b == 0:
                        link(ve.memset(ub[:, c, HALF + 1:HALF + 2], 0.0))
                    ve.tensor_tensor(ub[:, c, c0:c0 + n], csb[:, c, 0:n], bank[:, 0:n], ALU.mult).then_inc(B_free, 1)
                    dve.wait_ge(B_free, n_of(*pieces[1]))
                    w = [vec[:, V_CONV + 4 * j + ch:V_CONV + 4 * j + ch + 1] for j in range(3)]
                    yc = y[1][:, ch, :]
                    if f == 1 and ch == 0:
                        settle()
                    link(ve.tensor_scalar(yc, ub[:, c, 0:HALF], w[0], None, ALU.mult))
                    for j in (1, 2):
                        link(ve.scalar_tensor_tensor(out=yc, in0=ub[:, c, j:j + HALF], scalar=w[j], in1=yc,
                                                     op0=ALU.mult, op1=ALU.add))
                    bank = turn_in(*pieces[2])
                    link(ve.tensor_tensor(yc, yc, bank[:, 0:HALF], ALU.mult))
                    dve.sem_inc(B_free, 1)
                    dve.sem_inc(y1_done, 1)
                elif kind == "att":
                    _, f, h = step
                    u = H * f + h
                    dve.wait_ge(lg_made, u + 1)
                    link(ve.tensor_reduce(tiny[:, 2:4], scb[:, :].rearrange("p (t m) -> p t m", t=TPH), AX_X, ALU.max))
                    if u:
                        dve.wait_ge(pexp, TPH * u)
                    ve.tensor_scalar(tiny[:, 0:2], tiny[:, 2:4], -float(P) ** -0.5, None, ALU.mult).then_inc(mx_done, 1)
                    dve.wait_ge(pexp, TPH * (u + 1))
                    link(ve.reciprocal(tiny[:, 6:8], tiny[:, 4:6]))
                    for t in range(TPH):
                        ins = ve.tensor_scalar(prob[:, t, :], prob[:, t, :], tiny[:, 6 + t:7 + t], None, ALU.mult)
                        tick(ins) if t == 0 else ins.then_inc(pnorm, 1)
                elif kind == "branch":
                    _, f, n, b = step
                    for c in range(2):
                        dc = 2 * b + c
                        dve.wait_ge(A_free, n_of(*pieces[2 * c]))
                        bank = turn_in(*pieces[2 * c + 1])
                        if n == BRANCH_ORDER[0]:
                            ve.tensor_tensor(merged[:, dc, :], gsb[:, c, :], bank[:, 0:HALF], ALU.mult).then_inc(B_free, 1)
                        else:
                            link(ve.tensor_tensor(gsb[:, c, :], gsb[:, c, :], bank[:, 0:HALF], ALU.mult))
                            ve.tensor_tensor(merged[:, dc, :], merged[:, dc, :], gsb[:, c, :], ALU.add).then_inc(B_free, 1)
                elif kind == "hg":
                    _, f, b = step
                    for c in range(2):
                        h = 2 * b + c
                        dve.wait_ge(A_free, n_of(*pieces[2 * c + 1]))
                        link(ve.reciprocal(gsb[:, c, :], gsb[:, c, :]))
                        link(ve.scalar_tensor_tensor(out=gsb[:, c, :], in0=oT[:, h, f * HALF:(f + 1) * HALF],
                                                     scalar=vec[:, V_HG + h:V_HG + h + 1], in1=gsb[:, c, :],
                                                     op0=ALU.mult, op1=ALU.mult))
                        ve.tensor_tensor(y[0][:, h, :], gsb[:, c, :], csb[:, c, 0:HALF], ALU.mult).then_inc(y0_done, 1)
                elif kind == "wout":
                    _, f, b = step
                    for t in range(TPH):
                        bank = turn_in(*pieces[t])
                        dve.wait_ge(x_nat, 16 * TPH * (f + 1))
                        cols = slice(b * WCOLS, (b + 1) * WCOLS)
                        ve.tensor_tensor(x2[:, t, cols], x2[:, t, cols], bank[:, 0:WCOLS], ALU.add).then_inc(B_free, 1)
                elif kind == "ffn":
                    f = step[1]
                    dve.wait_ge(late_in, 48)
                    for t in range(TPH):
                        dve.wait_ge(ssq_done, TPH * f + t + 1)
                        link(ve.reciprocal(tiny[:, 12 + t:13 + t], tiny[:, 10 + t:11 + t]))
                        ve.scalar_tensor_tensor(out=h2[:, TPH * f + t, :], in0=x2[:, t, :], scalar=tiny[:, 12 + t:13 + t],
                                                in1=g_ffn[:, :], op0=ALU.mult, op1=ALU.mult).then_inc(h2_done, 1)
                elif kind == "best":
                    _, t, g = step
                    f, tl = t // TPH, t % TPH
                    dve.wait_ge(A_free, n_of("A", ("pq", f, 2 * g + 1, "s", 1)))
                    hps = range(2 * HQ * g, 2 * HQ * (g + 1))
                    hs = range(HQ * g, HQ * (g + 1))
                    sc = lambda hp: score[:, tl, hp * NK:hp * NK + NK]

                    def best16(items, value, where, source):
                        for o_ in (0, 8):
                            settle()
                            for i in items:
                                tick(ve.max(value[:, i, o_:o_ + 8], source(i)))
                            settle()
                            for i in items:
                                tick(ve.max_index(where[:, i, o_:o_ + 8], value[:, i, o_:o_ + 8], source(i)))
                            if o_ == 0:
                                settle()
                                for i in items:
                                    tick(ve.match_replace(source(i), value[:, i, 0:8], source(i), NEG))

                    best16(hps, tv, ti, sc)
                    settle()
                    a0, a1 = hps[0], hps[-1] + 1
                    h0, h1 = hs[0], hs[-1] + 1
                    dve.sem_inc(top1_done, 1)
                    link(ve.tensor_copy(tif[:, a0:a1, :], ti[:, a0:a1, :]))
                    tif4 = tif[:, a0:a1, :].rearrange("p (h s) k -> p h s k", s=2)
                    tv4 = tv[:, a0:a1, :].rearrange("p (h s) k -> p h s k", s=2)
                    link(ve.tensor_scalar(tif4[:, :, 0, :], tif4[:, :, 0, :], float(NK), None, ALU.mult))
                    for dst, s4 in ((cs, tv4), (ci, tif4)):
                        off = 0
                        for i0, ni, nj in CAND_ROWS:
                            o_ = dst[:, h0:h1, off:off + ni * nj].rearrange("p h (i j) -> p h i j", i=ni)
                            tick(ve.tensor_tensor(o_, s4[:, :, 0, i0:i0 + ni].unsqueeze(3).to_broadcast([P, HQ, ni, nj]),
                                                  s4[:, :, 1, 0:nj].unsqueeze(2).to_broadcast([P, HQ, ni, nj]), ALU.add))
                            off += ni * nj
                    if QH * t + g:
                        dve.wait_ge(gate_done, QH * t + g)
                    best16(hs, bs, pos, lambda h: cs[:, h, :])
                elif kind == "look":
                    _, t, g = step
                    h0, h1 = HQ * g, HQ * (g + 1)
                    bq, pq_ = bs[:, h0:h1, :], posf[:, h0:h1, :]
                    settle()
                    if QH * t + g:
                        dve.wait_ge(idx_done, QH * t + g)
                    tick(ve.tensor_copy(pq_, pos[:, h0:h1, :]))
                    link(ve.tensor_copy(tiny[:, 24 + h0:24 + h1], bs[:, h0:h1, 0]))
                    ve.tensor_tensor(bq, bq, tiny[:, 24 + h0:24 + h1].unsqueeze(2).to_broadcast([P, HQ, TOP]),
                                     ALU.subtract).then_inc(gd_done, 1)
                    iota = cst[:, C_IOTA:C_IOTA + NCAND].unsqueeze(1).to_broadcast([P, TOP, NCAND])
                    for h in range(h0, h1):
                        link(ve.tensor_tensor(eq[:, :, :], iota, posf[:, h, :].unsqueeze(2).to_broadcast([P, TOP, NCAND]),
                                              ALU.is_equal))
                        link(ve.tensor_tensor(eq[:, :, :], eq[:, :, :], ci[:, h, :].unsqueeze(1).to_broadcast([P, TOP, NCAND]),
                                              ALU.mult))
                        link(ve.tensor_reduce(posf[:, h, :], eq[:, :, :], AX_X, ALU.add))
                    ve.tensor_copy(idx[:, t, h0 * TOP:h1 * TOP], pq_.rearrange("p h k -> p (h k)")).then_inc(idx_done, 1)
                    dve.wait_ge(ge_done, QH * t + g + 1)
                    link(ve.tensor_reduce(tiny[:, 24 + h0:24 + h1], bq, AX_X, ALU.add))
                    link(ve.reciprocal(tiny[:, 24 + h0:24 + h1], tiny[:, 24 + h0:24 + h1]))
                    ve.tensor_tensor(gate[:, t, h0 * TOP:h1 * TOP].rearrange("p (h k) -> p h k", h=HQ), bq,
                                     tiny[:, 24 + h0:24 + h1].unsqueeze(2).to_broadcast([P, HQ, TOP]),
                                     ALU.mult).then_inc(gate_done, 1)
                elif kind == "gather":
                    _, t, k, n = step
                    whole = n // RING
                    if whole > 1:
                        with dve.Fori(0, whole) as it:
                            dots(t, k, RING, it)
                    else:
                        whole = 0
                    dots(t, k + whole * RING, n - whole * RING, 0)
                elif kind == "drain":
                    t = step[1]
                    dve.wait_ge(back_in, 16 * (t + 1))
                    dve.wait_ge(used, RING + (t + 1) * SLOTS)
                    ve.tensor_tensor(h2[:, t, :], h2[:, t, :], wide[:, :], ALU.add).then_inc(drained, 1)
                elif kind == "last":
                    t = step[1]
                    dve.wait_ge(fsq, t + 1)
                    link(ve.reciprocal(tiny[:, 18:19], tiny[:, 17:18]))
                    ve.scalar_tensor_tensor(out=h2[:, t, :], in0=h2[:, t, :], scalar=tiny[:, 18:19], in1=g_fin[:, :],
                                            op0=ALU.mult, op1=ALU.mult).then_inc(fdone, 1)


def kernel(**inp):
    import numpy as _np
    import concourse.bacc as _bacc
    from concourse.bass_utils import run_bass_kernel_spmd as _run

    def cols(v_):
        return _np.asarray(v_).reshape(-1, P).T

    g = {k: _np.asarray(v_) for k, v_ in inp.items()}
    vec = _np.concatenate([cols(g["norm_mix_g"][0]), cols(g["mem_norm_g"][0]), cols(g["hg_lb"][0].reshape(-1)),
                           cols(g["hg_lb"][1].reshape(-1)), cols(g["hg_norm_g"][0]), cols(g["sc_conv_w"][0].reshape(-1))], axis=1)
    arrays = {
        "xT": g["x"][0].T, "x": g["x"][0], "memT": g["mem"][0].T, "cst": constants()[0], "hcst": constants()[1], "vec": vec,
        "w_in": g["w_in"][0], "w_kv": g["w_mem_kv"][0], "w_br": g["w_branch"][0].reshape(3 * BW, D),
        "w_out": g["w_out"][0], "w_pq": g["peer_w_q"][0],
        "keys": g["peer_sub_keys"][0].reshape(HP, NK, P).transpose(2, 0, 1).reshape(P, HP * NK),
        "g_ffn": _np.broadcast_to(g["norm_ffn_g"][0], (P, D)), "g_fin": _np.broadcast_to(g["final_norm_g"], (P, D)),
        "uv": _np.concatenate([g["peer_u"][0], g["peer_v"][0]], axis=1),
    }
    arrays = {k: _np.ascontiguousarray(v_) for k, v_ in arrays.items()}
    nc = _bacc.Bacc("TRN2", target_bir_lowering=False, num_devices=1)
    args = {k: nc.dram_tensor(f"in_{k}", v_.shape, F32, kind="ExternalInput").ap() for k, v_ in arrays.items()}
    out = nc.dram_tensor("out_y", (1, T, D), F32, kind="ExternalOutput").ap()
    build(nc, args, out)
    r = _run(nc, [{f"in_{k}": v_ for k, v_ in arrays.items()}], core_ids=[0])
    return r.results[0]["out_y"]
```

```python
from contextlib import ExitStack

import numpy as np

import concourse.bass as bass
from concourse import mybir

F32 = mybir.dt.float32
U32 = mybir.dt.uint32
BF16 = mybir.dt.bfloat16
ALU = mybir.AluOpType
ACT = mybir.ActivationFunctionType
AX_X = mybir.AxisListType.X

P = 128
T = 512
D = 1024
KD = D // P
NT = T // P
HALF = 256
TPH = HALF // P
HALVES = T // HALF
NMEM = 256
H = 4
CH = 64
NCH = T // CH
BW = 512
BC = BW // P
EPS = 1e-6
NEG = -3.0e38
HP = 16
PH = 8
NK = 128
TOP = 16
SLOTS = PH * TOP
RING = 6
GROUP = 2
QH = 8
HQ = PH // QH
SHARE = {"best": 2.5, "look": 2.5, "conv": 2.6, "mq": 2.6, "branch": 3.2, "logits": 2.8, "norm_att": 0.0,
         "values": 2.8, "hg": 3.4, "turn_p": 2.8, "hg_mul": 0.0, "wout": 2.6, "ffn": 2.0, "turn": 1.5, "query": 2.6, "keys": 1.0}
GROUP_SLOTS = (9, 10)
EARLY_END = 122
WSLOTS = 4
WCOLS = 256
CAND_ROWS = ((0, 1, 16), (1, 1, 8), (2, 1, 5), (3, 1, 4), (4, 4, 3), (8, 8, 1))
NCAND = sum(ni * nj for _, ni, nj in CAND_ROWS)
COL_Q, COL_V, COL_F, COL_B, COL_HG, COL_SB, COL_SC, COL_SH, COL_MQ, COL_GATE = (BW * i for i in range(10))
C_ID, C_ONE, C_IOTA = 0, 128, 256
C_N = C_IOTA + NCAND
S_MF, S_MB, S_KEEP = 0, 128, 256
S_N = S_KEEP + T
V_MIX, V_MEM, V_LB, V_HG, V_CONV = 0, 8, 16, 32, 36
V_N = 48
BRANCH_ORDER = (1, 2, 0)


def constants():
    c, m = np.zeros((P, C_N), np.float32), np.zeros((P, S_N), np.float32)
    c[:, C_ID:C_ID + P] = np.eye(P)
    c[:, C_ONE:C_ONE + P] = 1.0
    s, t = np.arange(P)[:, None], np.arange(P)[None, :]
    same = s // CH == t // CH
    m[:, S_MF:S_MF + P] = same & (s <= t)
    m[:, S_MB:S_MB + P] = same & (s >= t)
    m[:, S_KEEP:S_KEEP + T] = np.arange(T) % CH != 0
    c[:, C_IOTA:] = np.arange(NCAND)
    return c, m


def plan():
    steps = [("norm_mem",), ("square_in",), ("kv", 0), ("norm_in",), ("kv", 1), ("kv", 2), ("kv", 3)]
    steps += [("z", d, b) for d in range(2) for b in range(2)]
    steps += [("q", b) for b in range(2)] + [("v", b) for b in range(2)]

    def mixers(f):
        conv = [("conv", f, ch // 2, ch % 2, w) for ch in range(BC) for w in "ChB"]
        mq = [("mq", f, h // 2, h % 2) for h in range(H)]
        att = [("logits", f, 0)]
        for h in range(H):
            att += [("norm_att", f, h), ("hg", f, h // 2, h % 2), ("turn_p", f, h)]
            att += [("logits", f, h + 1)] if h + 1 < H else []
            att += [("hg_mul", f, h), ("values", f, h)]
        br = {n: [("branch", f, n, b, c) for b in range(4) for c in range(2)] for n in range(3)}
        return conv, mq, att, br

    def tail(f):
        return [("wout", f, b, t) for b in range(4) for t in range(TPH)] + [("ffn", f)], \
            [("turn", f, t) for t in range(TPH)]

    def scores(f, g):
        return [s for b in range(HQ * g, HQ * (g + 1)) for s in (("query", f, b, 0), ("query", f, b, 1), ("keys", f, b))]

    def topk(t, g):
        return [("best", t, g), ("look", t, g)]

    conv, mq, att, br = mixers(0)
    side = conv + mq + br[1]
    for s in [("logf",)] + [s for h in range(H) for s in (("elem", h, 0), ("elem", h, 1), *["side"] * 4, ("intra", h, 0),
                                                          "side", ("intra", h, 1), "side", ("o", h))]:
        if s != "side":
            steps.append(s)
        elif side:
            steps.append(side.pop(0))
    end, turns = tail(0)
    steps += side + att + br[2] + br[0] + end
    steps.append(("open", 0))
    steps += turns + scores(0, 0) + [("best", 0, 0)] + scores(0, 1) + [("look", 0, 0)] + scores(0, 2)

    def mixed(main, other):
        return [s for pair in zip(main, other) for s in pair] + other[len(main):]

    first = [topk(0, g) + (scores(0, g + 2) if g + 2 < QH else []) for g in range(1, QH)]
    conv, mq, att, br = mixers(1)
    end, turns = tail(1)
    early = mixed(conv, [s for g in range(QH) for s in topk(1, g)])
    for h in range(H):
        att.insert(att.index(("logits", 1, 0)) if h == 0 else att.index(("norm_att", 1, h - 1)), mq[h])
    rest = att + br[1] + br[2] + br[0] + end + turns + scores(1, 0) + topk(2, 0)
    more = [[s for s in scores(1, g) + topk(2, g)] for g in range(1, QH)]
    more.append([s for g in range(QH) for s in topk(3, g)])
    slot = 0
    pending = []

    def gather(n):
        nonlocal slot
        while n > 0:
            t, k = divmod(slot, SLOTS)
            m = min(n, SLOTS - k)
            steps.append(("gather", t, k, m))
            slot, n = slot + m, n - m
            if pending and [s[0] for s in steps if s[0] not in ("gather", "drain", "open", "last", "store")][-1] != "query":
                steps.extend(pending.pop(0))
            if k + m == SLOTS:
                steps.append(("drain", t))
                if t + 1 < NT:
                    steps.append(("open", t + 1))
                    pending.extend([[], [("last", t)], [("store", t)]])
                else:
                    steps.extend([("last", t), ("store", t)])

    def spread(todo, until):
        start, done, whole = slot, 0.0, sum(SHARE[s[0]] for s in todo)
        for s in todo:
            done += SHARE[s[0]]
            n = round(done / whole * (until - start)) + start - slot
            gather(min(n - n % 2, 4))
            steps.append(s)

    for g in range(1, QH):
        spread(first[g - 1], GROUP_SLOTS[0] * g)
    spread(early, EARLY_END)
    spread(rest, TPH * SLOTS - 4)
    gather(TPH * SLOTS - slot)
    for g in range(1, QH):
        spread(more[g - 1], TPH * SLOTS + GROUP_SLOTS[1] * g)
    spread(more[-1], (TPH + 1) * SLOTS - 4)
    for t in range(NT):
        for g in range(QH):
            seen = sum(s[3] for s in steps[:steps.index(("look", t, g))] if s[0] == "gather")
            assert seen <= t * SLOTS + g * (SLOTS // QH), (t, g, seen)
    assert all(steps.index(("best", 1, g)) < steps.index(("mq", 1, 0, 0)) for g in range(QH))
    assert steps.index(("open", 1)) < steps.index(("wout", 1, 0, 0))
    while slot < NT * SLOTS:
        gather(RING if pending else SLOTS - slot % SLOTS)
    return steps


def tensor_order(steps):
    steps = [s for s in steps if s[0] not in ("best", "look")]
    i = 0
    while i < len(steps) - 1:
        a, b = steps[i:i + 2]
        if a[0] == "gather" and a[3] <= RING and (chunks_of(b) or b[0] in ("logits", "turn_p", "values")):
            steps[i:i + 2] = b, a
            i += 1
        i += 1
    return steps


def chunks_of(step):
    k = step[0]
    if k in ("norm_in", "norm_mem"):
        return [("B" if k == "norm_in" else "A", step)]
    if k == "kv":
        return [("A", (*step, c)) for c in range(2)]
    if k in ("z", "q"):
        return [("A", (*step, c)) for c in range(2)]
    if k == "v":
        return [("A", (*step, t)) for t in range(NT)]
    if k == "conv":
        return [("A" if step[4] == "C" else "B", step)]
    if k in ("mq", "query"):
        return [("A", step)]
    if k == "branch":
        return [("A", (*step, "gate")), ("B", (*step, "br"))]
    if k == "hg":
        return [("A", (*step, "z")), ("A", (*step, "ss"))]
    if k == "wout":
        return [("B", step)]
    if k in ("turn", "keys"):
        return [("A", (*step, g)) for g in range(2)]
    return []


def weights_of(step):
    k = step[0]
    if k == "kv":
        return [("kv", 0, D, WCOLS * step[1], WCOLS)]
    if k == "z":
        return [("in", 0, D, (COL_F, COL_B)[step[1]] + WCOLS * step[2], WCOLS)]
    if k == "q":
        return [("in", 0, D, COL_Q + WCOLS * step[1], WCOLS)]
    if k == "v":
        return [("in", 0, D, COL_V + WCOLS * step[1], WCOLS)]
    if k == "conv":
        return [("in", 0, D, {"C": COL_SC, "h": COL_SH, "B": COL_SB}[step[4]] + WCOLS * step[2], WCOLS)]
    if k == "mq":
        return [("in", 0, D, COL_MQ + WCOLS * step[2], WCOLS)]
    if k == "hg":
        return [("in", 0, D, COL_HG + WCOLS * step[2], WCOLS)]
    if k == "branch":
        _, _, n, b, _ = step
        return [("in", 0, D, COL_GATE + D * n + WCOLS * b, WCOLS), ("br", BW * n, BW, WCOLS * b, WCOLS)]
    if k == "wout":
        return [("out", 0, D, WCOLS * step[2], WCOLS)]
    if k == "query":
        return [("pq", 0, D, WCOLS * step[2], WCOLS)]
    return []


def build(nc, a, out):
    steps = plan()
    order = {"A": [], "B": []}
    blocks, block_of = [], {}
    block_end = []
    numbers = {}
    for s in steps:
        order_of_step = chunks_of(s)
        for r, key in order_of_step:
            order[r].append(key)
        for i, w in enumerate(weights_of(s)):
            half = s[1] if len(s) > 1 and s[0] not in ("kv", "z", "q", "v") else None
            b = numbers.setdefault((half, w), len(blocks))
            if b == len(blocks):
                blocks.append(w)
                block_end.append(None)
            block_of[s, i] = b
            block_end[b] = order_of_step[-1]
    place = {r: {key: i for i, key in enumerate(o)} for r, o in order.items()}

    with ExitStack() as ctx:
        def sb(name, shape, dt=F32):
            return ctx.enter_context(nc.sbuf_tensor(name, shape, dt))

        def sem(name):
            return ctx.enter_context(nc.semaphore(name))

        cst = sb("cst", [P, C_N])
        ident, ones = cst[:, C_ID:C_ID + P], cst[:, C_ONE:C_ONE + P]
        vec = sb("vec", [P, V_N])
        lbs = sb("lbs", [P, 3, 8])
        eps = sb("eps", [P, 1])
        keys = sb("keys", [P, HP * NK])
        g_ffn = sb("g_ffn", [P, D])
        g_fin = sb("g_fin", [P, D])
        hT = sb("hT", [P, KD, T])
        W = sb("W", [P, WSLOTS, KD * WCOLS])
        mkT = sb("mkT", [P, H, NMEM])
        mv = sb("mv", [P, NMEM // P, BW])
        oT = sb("oT", [P, H, T])
        ys = sb("ys", [P, 4096])
        y = [ys[:, n * BC * HALF:(n + 1) * BC * HALF].rearrange("p (c t) -> p c t", c=BC) for n in range(3)]
        score = ys[:, :].rearrange("p (t k) -> p t k", t=TPH)
        mx = sb("mx", [P, KD * HALF])
        merged = mx[:, :].rearrange("p (k t) -> p k t", k=KD)
        mqT = y[2]
        prob = ys[:, 3 * BC * HALF:3 * BC * HALF + 512].rearrange("p (t m) -> p t m", t=TPH)
        probT = ys[:, 3 * BC * HALF + 512:4096].rearrange("p (m t) -> p m t", m=2)
        WIN = HALF + 1
        csb = sb("csb", [P, 2, WIN])
        ub = sb("ub", [P, 2, HALF + 2])
        gsb = sb("gsb", [P, 2, HALF])
        tmp = sb("tmp", [P, 2, HALF])
        qpT = sb("qpT", [P, 2, HALF])
        tiny = sb("tiny", [P, 32])
        acts = sb("acts", [P, 3, RING])
        stage = sb("stage", [P, RING, 1], U32)
        diag = sb("diag", [P, RING, P])
        junk = qpT[:, :, :].rearrange("p c t -> p (c t)").bitcast(BF16)
        AR = RING * 2 * D + NT * D + TPH * D + 3 * HP * TOP + 2 * PH * NCAND + 3 * SLOTS + TOP * NCAND + 2 * NT * SLOTS
        arena = sb("arena", [P, AR])
        at = [0]

        def cut(n):
            at[0] += n
            assert at[0] <= AR, at[0]
            return arena[:, at[0] - n:at[0]]

        sig = cut(2 * H * T).rearrange("p (d h t) -> p d h t", d=2, h=H)
        sgn = cut(2 * H * T).rearrange("p (d h t) -> p d h t", d=2, h=H)
        sqx = arena[:, 0:KD * T].rearrange("p (k t) -> p k t", k=KD)
        memT = arena[:, KD * T:KD * T + KD * NMEM].rearrange("p (k t) -> p k t", k=KD)
        sqm = arena[:, KD * T + KD * NMEM:KD * T + 2 * KD * NMEM].rearrange("p (k t) -> p k t", k=KD)
        qT = cut(H * T).rearrange("p (h t) -> p h t", h=H)
        v = cut(NT * BW).rearrange("p (t e) -> p t e", t=NT)
        cumG, dref, expn, dlast = ([cut(T) for _ in range(2)] for _ in range(4))
        kdn = [cut(NT * 2 * P).rearrange("p (j i d) -> p j i d", j=NT, i=2) for _ in range(2)]
        PT = [cut(NT * P) for _ in range(2)]
        state = [cut(NCH * P).rearrange("p (n e) -> p n e", n=NCH) for _ in range(2)]
        decay = [cut(NCH) for _ in range(2)]
        hcst = cut(S_N)
        at[0] = 0
        ring = cut(RING * 2 * D).rearrange("p (s n) -> p s n", s=RING)
        h2 = cut(NT * D).rearrange("p (t n) -> p t n", t=NT)
        x2 = cut(TPH * D).rearrange("p (t n) -> p t n", t=TPH)
        tv, tif = (cut(HP * TOP).rearrange("p (s k) -> p s k", s=HP) for _ in range(2))
        ti = cut(HP * TOP).bitcast(U32).rearrange("p (s k) -> p s k", s=HP)
        cs, ci = (cut(PH * NCAND).rearrange("p (h c) -> p h c", h=PH) for _ in range(2))
        bs, posf = (cut(SLOTS).rearrange("p (h k) -> p h k", h=PH) for _ in range(2))
        pos = cut(SLOTS).bitcast(U32).rearrange("p (h k) -> p h k", h=PH)
        eq = cut(TOP * NCAND).rearrange("p (k c) -> p k c", k=TOP)
        gate = cut(NT * SLOTS).rearrange("p (t s) -> p t s", t=NT)
        idx = cut(NT * SLOTS).bitcast(U32).rearrange("p (t s) -> p t s", t=NT)
        banks = [ctx.enter_context(nc.psum_tensor(f"bank{i}", [P, 512], F32)) for i in range(6)]
        wide = ctx.enter_context(nc.psum_tensor("wide", [P, 1024], F32))
        bankA, bankB = banks[0:2], banks[2:4]
        tp, scb = banks[4], banks[5]

        x_in, c_in, mem_in, late_in = sem("x_in"), sem("c_in"), sem("mem_in"), sem("late_in")
        hc_in = sem("hc_in")
        w_in = [sem(f"w_in{i}") for i in range(WSLOTS)]
        A_full, A_free = sem("A_full"), sem("A_free")
        B_full, B_free = sem("B_full"), sem("B_free")
        v_ord, a_ord = sem("v_ord"), sem("a_ord")
        sq_done, root, eps_done, lb_exp = sem("sq_done"), sem("root"), sem("eps_done"), sem("lb_exp")
        h_done, m_done = sem("h_done"), sem("m_done")
        lb_done = sem("lb_done")
        zero_done = sem("zero_done")
        logf_done = sem("logf_done")
        dsub, exps, prods = sem("dsub"), sem("exps"), sem("prods")
        kd_turned, kd_copied = sem("kd_turned"), sem("kd_copied")
        sc_made, sc_masked = sem("sc_made"), sem("sc_masked")
        ds_made, st_done = sem("ds_made"), sem("st_done")
        o_made, o_kept = sem("o_made"), sem("o_kept")
        y1_done = sem("y1_done")
        lg_made, mx_done, pexp, pnorm = sem("lg_made"), sem("mx_done"), sem("pexp"), sem("pnorm")
        p_turned, pT_done, pv_made, y2_done = sem("p_turned"), sem("pT_done"), sem("pv_made"), sem("y2_done")
        osq_done, y0_done = sem("osq_done"), sem("y0_done")
        x_nat, opened = sem("x_nat"), sem("opened")
        ssq_done, h2_done = sem("ssq_done"), sem("h2_done")
        gd_done, ge_done, idx_done, gate_done = sem("gd_done"), sem("ge_done"), sem("idx_done"), sem("gate_done")
        landed = [sem(f"landed{i}") for i in range(RING)]
        staged, seen = sem("staged"), sem("seen")
        dot, gel, wgt, dia, used = sem("dot"), sem("gel"), sem("wgt"), sem("dia"), sem("used")
        drained, fsq, fdone, out_done = sem("drained"), sem("fsq"), sem("fdone"), sem("out_done")
        top1_done, lb_diff = sem("top1_done"), sem("lb_diff")
        last_before_hg = {}
        for f in range(HALVES):
            before = steps[:steps.index(("hg", f, 0, 0))]
            last_before_hg[f] = [key for s in before for r, key in chunks_of(s) if r == "B"][-1]

        full = {"A": A_full, "B": B_full}
        free = {"A": A_free, "B": B_free}

        def n_of(r, key):
            return place[r][key] + 1

        def bank_of(r, key):
            return (bankA if r == "A" else bankB)[place[r][key] % 2]

        def wblock(step, i):
            b = block_of[step, i]
            kc = blocks[b][2] // P
            return W[:, b % WSLOTS, 0:kc * WCOLS].rearrange("p (k n) -> p k n", k=kc)

        def window(f):
            return (0, 0 + HALF + 1, 1) if f == 0 else (HALF - 1, HALF + 1, 0)

        src = {"in": a["w_in"], "kv": a["w_kv"], "br": a["w_br"], "out": a["w_out"], "pq": a["w_pq"]}
        xn = a["x"].rearrange("(t p) n -> t p n", p=P)
        outn = out.rearrange("b (t p) n -> (b t) p n", p=P)

        def land_count(g):
            return 16 * (g // RING + 1)

        block = ctx.enter_context(nc.Block())

        @block.sync
        def _(sp):
            def load_block(b):
                name, r0, rows, c0, cols = blocks[b]
                kc = rows // P
                sp.dma_start(W[:, b % WSLOTS, 0:kc * cols].rearrange("p (k n) -> p k n", k=kc),
                             src[name][r0:r0 + rows, c0:c0 + cols].rearrange("(k p) n -> p k n", p=P))\
                  .then_inc(w_in[b % WSLOTS], 16)

            sp.dma_start(memT, a["memT"].rearrange("(k p) t -> p k t", p=P)).then_inc(mem_in, 16)
            sp.dma_start(cst[:, :], a["cst"]).then_inc(c_in, 16)
            sp.dma_start(vec[:, :], a["vec"]).then_inc(c_in, 16)
            load_block(0)
            xT_v = a["xT"].rearrange("(k p) t -> p k t", p=P)
            for i in range(4):
                sp.dma_start(hT[:, 2 * i:2 * i + 2, :], xT_v[:, 2 * i:2 * i + 2, :]).then_inc(x_in, 16)
            xload_at = {block_of[("wout", f, 0, 0), 0]: f for f in range(HALVES)}
            for b in range(1, len(blocks)):
                if b >= WSLOTS:
                    r, key = block_end[b - WSLOTS]
                    sp.wait_ge(full[r], n_of(r, key))
                load_block(b)
                if b == 5:
                    sp.dma_start(hcst, a["hcst"]).then_inc(hc_in, 16)
                    sp.dma_start(keys[:, :], a["keys"]).then_inc(late_in, 16)
                    sp.dma_start(g_ffn[:, :], a["g_ffn"]).then_inc(late_in, 16)
                    sp.dma_start(g_fin[:, :], a["g_fin"]).then_inc(late_in, 16)
                if b in xload_at:
                    f = xload_at[b]
                    if f == 0:
                        sp.wait_ge(o_kept, H)
                    else:
                        sp.wait_ge(opened, TPH * f)
                        sp.wait_ge(h2_done, TPH * f)
                    for t in range(TPH):
                        sp.dma_start(x2[:, t, :], xn[TPH * f + t]).then_inc(x_nat, 16)
            sp.wait_ge(out_done, 16 * NT)

        @block.gpsimd
        def _(pool):
            def issue(t, k, s, it):
                g = t * SLOTS + k
                pool.wait_ge(used, it * RING + (g + 1))
                col = idx[:, t, bass.ds(it * RING + k, 1)] if not isinstance(it, int) else idx[:, t, k:k + 1]
                nc.gpsimd.tensor_copy(stage[:, s, :], col).then_inc(staged, 1)
                pool.wait_ge(staged, it * RING + (g + 1))
                pool.sem_inc(seen, 1)
                pool.indirect_dma_start(ring[:, s, :], None, a["uv"],
                                        bass.IndirectOffsetOnAxis(ap=stage[:, s, :], axis=0)).then_inc(landed[s], 16)

            n = SLOTS // QH
            for t in range(NT):
                for g in range(QH):
                    pool.wait_ge(idx_done, QH * t + g + 1)
                    k = n * g
                    with pool.Fori(0, n // RING) as it:
                        for i in range(RING):
                            issue(t, k + i, (t * SLOTS + k + i) % RING, it)
                    for i in range(n // RING * RING, n):
                        issue(t, k + i, (t * SLOTS + k + i) % RING, 0)

        @block.tensor
        def _(pe):
            mm = nc.tensor.matmul

            def open_piece(r, key):
                n = n_of(r, key)
                if n > 2:
                    pe.wait_ge(free[r], n - 2)
                return bank_of(r, key)

            def need_weights(step, i):
                b = block_of[step, i]
                pe.wait_ge(w_in[b % WSLOTS], 16 * (b // WSLOTS + 1))
                return wblock(step, i)

            def project(r, key, outp, lhs, rhs, kc=KD):
                for k in range(kc):
                    last = mm(outp, lhs(k), rhs(k), start=(k == 0), stop=(k == kc - 1))
                last.then_inc(full[r], 1)

            def products(t, k, s, it):
                g = t * SLOTS + k
                pe.wait_ge(dia, it * RING + (g + 1))
                for c in range(2):
                    last = mm(wide[:, 512 * c:512 * c + 512], diag[:, s, :], ring[:, s, D + 512 * c:D + 512 * c + 512],
                              start=False, stop=False, skip_group_check=True)
                last.then_inc(used, 1)

            for step in tensor_order(steps):
                kind = step[0]
                pieces = chunks_of(step)
                if kind in ("norm_in", "norm_mem"):
                    bank = open_piece(*pieces[0])
                    sq, n, c0 = (sqx, T, KD) if kind == "norm_in" else (sqm, NMEM, 0)
                    pe.wait_ge(c_in, 32)
                    for k in range(KD):
                        pe.wait_ge(sq_done, c0 + k + 1)
                        last = mm(bank[:, 0:n], ones, sq[:, k, :], start=(k == 0), stop=(k == KD - 1))
                    last.then_inc(full[pieces[0][0]], 1)
                elif kind == "kv":
                    b = step[1]
                    w = need_weights(step, 0)
                    pe.wait_ge(m_done, KD)
                    for c in range(2):
                        r, key = pieces[c]
                        bank = open_piece(r, key)
                        if b < 2:
                            project(r, key, bank[:, 0:NMEM], lambda k: w[:, k, c * P:c * P + P], lambda k: memT[:, k, :])
                        else:
                            project(r, key, bank[:, 0:WCOLS], lambda k: memT[:, k, c * P:c * P + P], lambda k: w[:, k, :])
                elif kind in ("z", "q"):
                    w = need_weights(step, 0)
                    pe.wait_ge(h_done, KD)
                    for c in range(2):
                        r, key = pieces[c]
                        bank = open_piece(r, key)
                        project(r, key, bank[:, :], lambda k: w[:, k, c * P:c * P + P], lambda k: hT[:, k, :])
                elif kind == "v":
                    w = need_weights(step, 0)
                    for t in range(NT):
                        r, key = pieces[t]
                        bank = open_piece(r, key)
                        project(r, key, bank[:, 0:WCOLS], lambda k: hT[:, k, t * P:t * P + P], lambda k: w[:, k, :])
                elif kind == "conv":
                    _, f, b, c, which = step
                    t0, n = window(f)[:2] if which != "B" else (f * HALF, HALF)
                    w = need_weights(step, 0)
                    r, key = pieces[0]
                    bank = open_piece(r, key)
                    project(r, key, bank[:, 0:n], lambda k: w[:, k, c * P:c * P + P], lambda k: hT[:, k, t0:t0 + n])
                elif kind == "mq":
                    _, f, b, c = step
                    w = need_weights(step, 0)
                    r, key = pieces[0]
                    bank = open_piece(r, key)
                    project(r, key, bank[:, 0:HALF], lambda k: w[:, k, c * P:c * P + P],
                            lambda k: hT[:, k, f * HALF:(f + 1) * HALF])
                elif kind == "branch":
                    _, f, n, b, c = step
                    wg, wb = need_weights(step, 0), need_weights(step, 1)
                    done = {1: (y1_done, BC), 2: (y2_done, H), 0: (y0_done, H)}[n]
                    r, key = pieces[0]
                    bank = open_piece(r, key)
                    project(r, key, bank[:, 0:HALF], lambda k: wg[:, k, c * P:c * P + P],
                            lambda k: hT[:, k, f * HALF:(f + 1) * HALF])
                    r, key = pieces[1]
                    bank = open_piece(r, key)
                    pe.wait_ge(done[0], done[1] * (f + 1))
                    project(r, key, bank[:, 0:HALF], lambda k: wb[:, k, c * P:c * P + P],
                            lambda k: y[n][:, k, :], BC)
                elif kind == "hg":
                    _, f, b, c = step
                    w = need_weights(step, 0)
                    h = 2 * b + c
                    r, key = pieces[0]
                    bank = open_piece(r, key)
                    project(r, key, bank[:, 0:HALF], lambda k: w[:, k, c * P:c * P + P],
                            lambda k: hT[:, k, f * HALF:(f + 1) * HALF])
                    r, key = pieces[1]
                    bank = open_piece(r, key)
                    pe.wait_ge(osq_done, f * H + h + 1)
                    mm(bank[:, 0:HALF], ones, tmp[:, c, :], start=True, stop=True).then_inc(A_full, 1)
                elif kind == "intra":
                    _, h, d = step
                    u = 2 * h + d
                    pe.wait_ge(prods, 4 * u + 4)
                    if u >= 1:
                        pe.wait_ge(kd_copied, u)
                    if d == 0 and h >= 1:
                        pe.wait_ge(o_kept, h)
                    for j in range(NT):
                        last = nc.tensor.transpose(tp[:, j * P:j * P + P], dlast[d][:, j * P:j * P + P], ident)
                    last.then_inc(kd_turned, 1)
                    if u >= 1:
                        pe.wait_ge(sc_masked, u)
                    for j in range(NT):
                        cols = slice(j * P, j * P + P)
                        last = mm(scb[:, cols], expn[d][:, cols], dref[d][:, cols], start=True, stop=True)
                    last.then_inc(sc_made, 1)
                    pe.wait_ge(kd_copied, u + 1)
                    if u >= 1:
                        pe.wait_ge(st_done, u)
                    for n in range(NCH):
                        last = mm(wide[:, n * P:n * P + P], kdn[d][:, n // 2, n % 2, :],
                                  v[:, n // 2, h * P:h * P + P], start=True, stop=True)
                    last.then_inc(ds_made, 1)
                elif kind == "o":
                    h = step[1]
                    pe.wait_ge(sc_masked, 2 * h + 2)
                    pe.wait_ge(st_done, 2 * h + 2)
                    for j in range(NT):
                        cols = slice(j * P, j * P + P)
                        vj = v[:, j, h * P:h * P + P]
                        mm(tp[:, cols], vj, PT[0][:, cols], start=True, stop=False, skip_group_check=True)
                        last = mm(tp[:, cols], vj, PT[1][:, cols], start=False, stop=False, skip_group_check=True)
                        work = [(d, n) for n in (2 * j, 2 * j + 1) for d in range(2)
                                if not (d == 0 and n == 0) and not (d == 1 and n == NCH - 1)]
                        for d, n in work:
                            cc = slice(n * CH, n * CH + CH)
                            last = mm(tp[:, cc], state[d][:, n, :], cumG[d][:, cc], start=False,
                                      stop=(d, n) == work[-1], skip_group_check=True)
                    last.then_inc(o_made, 1)
                elif kind == "logits":
                    _, f, h = step
                    u = H * f + h
                    pe.wait_ge(A_free, n_of("A", ("mq", f, h // 2, h % 2)))
                    if u >= 1:
                        pe.wait_ge(pexp, TPH * u)
                    else:
                        pe.wait_ge(sc_masked, 2 * H)
                    for t in range(TPH):
                        last = mm(scb[:, t * NMEM:(t + 1) * NMEM], mqT[:, h, t * P:t * P + P], mkT[:, h, :],
                                  start=True, stop=True)
                    last.then_inc(lg_made, 1)
                elif kind == "turn_p":
                    _, f, h = step
                    u = H * f + h
                    if u >= 1:
                        pe.wait_ge(y2_done, u)
                    else:
                        pe.wait_ge(o_kept, H)
                    pe.wait_ge(pnorm, u + 1)
                    for m in range(2):
                        for t in range(TPH):
                            last = nc.tensor.transpose(tp[:, m * HALF + t * P:m * HALF + t * P + P],
                                                       prob[:, t, m * P:m * P + P], ident)
                    last.then_inc(p_turned, 1)
                elif kind == "values":
                    _, f, h = step
                    u = H * f + h
                    pe.wait_ge(pT_done, u + 1)
                    for m in range(2):
                        last = mm(tp[:, 0:HALF], mv[:, m, h * P:h * P + P], probT[:, m, :], start=(m == 0), stop=(m == 1))
                    last.then_inc(pv_made, 1)
                elif kind == "wout":
                    _, f, b, t = step
                    w = need_weights(step, 0)
                    pe.wait_ge(B_free, n_of("B", ("branch", f, BRANCH_ORDER[-1], 3, 1, "br")))
                    r, key = pieces[0]
                    bank = open_piece(r, key)
                    project(r, key, bank[:, 0:WCOLS], lambda k: merged[:, k, t * P:t * P + P], lambda k: w[:, k, :])
                elif kind == "turn":
                    _, f, t = step
                    for g, (r, key) in enumerate(pieces):
                        bank = open_piece(r, key)
                        pe.wait_ge(h2_done, TPH * f + t + 1)
                        for k in range(4):
                            last = nc.tensor.transpose(bank[:, k * P:k * P + P],
                                                       h2[:, TPH * f + t, (4 * g + k) * P:(4 * g + k + 1) * P], ident)
                        last.then_inc(A_full, 1)
                elif kind == "query":
                    _, f, b, c = step
                    w = need_weights(step, 0)
                    pe.wait_ge(A_free, n_of("A", ("turn", f, TPH - 1, 1)))
                    r, key = pieces[0]
                    bank = open_piece(r, key)
                    project(r, key, bank[:, 0:HALF], lambda k: w[:, k, c * P:c * P + P], lambda k: merged[:, k, :])
                elif kind == "keys":
                    _, f, b = step
                    pe.wait_ge(late_in, 48)
                    for c, (r, key) in enumerate(pieces):
                        hp = 2 * b + c
                        bank = open_piece(r, key)
                        pe.wait_ge(A_free, n_of("A", ("query", f, b, c)))
                        for t in range(TPH):
                            last = mm(bank[:, t * P:t * P + P], qpT[:, c, t * P:t * P + P], keys[:, hp * NK:hp * NK + NK],
                                      start=True, stop=True)
                        last.then_inc(A_full, 1)
                elif kind == "open":
                    t = step[1]
                    if t == 0:
                        pe.wait_ge(st_done, 2 * H)
                        pe.sem_inc(used, RING)
                    else:
                        pe.wait_ge(drained, t)
                    pe.wait_ge(B_free, n_of("B", ("wout", t // TPH, 3, TPH - 1)))
                    for c in range(2):
                        last = mm(wide[:, 512 * c:512 * c + 512], ident, x2[:, t % TPH, 512 * c:512 * c + 512],
                                  start=True, stop=False, skip_group_check=True)
                    last.then_inc(opened, 1)
                elif kind == "gather":
                    _, t, k, n = step
                    whole = n // RING
                    if whole > 1:
                        with pe.Fori(0, whole) as it:
                            for s in range(RING):
                                products(t, k + s, (t * SLOTS + k + s) % RING, it)
                    else:
                        whole = 0
                    for i in range(whole * RING, n):
                        products(t, k + i, (t * SLOTS + k + i) % RING, 0)

        @block.scalar
        def _(act):
            done = [0]
            af = nc.scalar.activation

            def then_wait(ins):
                done[0] += 1
                ins.then_inc(a_ord, 1)
                act.wait_ge(a_ord, done[0])

            def turn_in(r, key):
                act.wait_ge(full[r], n_of(r, key))
                return bank_of(r, key)

            def gather_body(t, k, n, it):
                g = t * SLOTS + k
                for c in range(0, n, GROUP):
                    m = min(GROUP, n - c)
                    act.wait_ge(dot, it * RING + (g + c + m))
                    s = (g + c) % RING
                    af(acts[:, 1, s:s + m], acts[:, 0, s:s + m], ACT.Gelu).then_inc(gel, 1)
                    act.wait_ge(gel, it * (RING // GROUP) + (g + c) // GROUP + 1)
                    for i in range(c, c + m):
                        s = (g + i) % RING
                        col = gate[:, t, k + i:k + i + 1] if isinstance(it, int) else gate[:, t, bass.ds(it * RING + (k + i), 1)]
                        af(acts[:, 2, s:s + 1], acts[:, 1, s:s + 1], ACT.Copy, scale=col).then_inc(wgt, 1)
                    act.wait_ge(wgt, it * RING + (g + c + m))
                    for i in range(c, c + m):
                        s = (g + i) % RING
                        af(diag[:, s, :], ident, ACT.Copy, scale=acts[:, 2, s:s + 1]).then_inc(dia, 1)

            for step in steps:
                kind = step[0]
                pieces = chunks_of(step)
                if kind in ("norm_in", "norm_mem"):
                    n = T if kind == "norm_in" else NMEM
                    if kind == "norm_mem":
                        act.wait_ge(mem_in, 16)
                        for k in range(KD):
                            af(sqm[:, k, :], memT[:, k, :], ACT.Square).then_inc(sq_done, 1)
                    act.wait_ge(eps_done, 1)
                    bank = turn_in(*pieces[0])
                    af(bank[:, 0:n], bank[:, 0:n], ACT.Sqrt, scale=1.0 / D, bias=eps[:, :]).then_inc(root, 1)
                    if kind == "norm_mem":
                        act.wait_ge(m_done, KD)
                        act.sem_inc(A_free, 1)
                    if kind == "norm_in":
                        act.wait_ge(lb_diff, 2)
                        af(lbs[:, 0:2, :], lbs[:, 0:2, :], ACT.Exp).then_inc(lb_exp, 1)
                elif kind == "square_in":
                    act.wait_ge(x_in, 64)
                    for k in range(KD):
                        af(sqx[:, k, :], hT[:, k, :], ACT.Square).then_inc(sq_done, 1)
                elif kind == "kv":
                    for c in range(2):
                        bank = turn_in(*pieces[c])
                        b = step[1]
                        dst = mkT[:, 2 * b + c, :] if b < 2 else mv[:, c, (b - 2) * WCOLS:(b - 1) * WCOLS]
                        af(dst, bank[:, 0:NMEM], ACT.Copy).then_inc(A_free, 1)
                elif kind == "z":
                    _, d, b = step
                    for c in range(2):
                        h = 2 * b + c
                        bank = turn_in(*pieces[c])
                        af(sig[:, d, h, :], bank[:, :], ACT.Sigmoid)
                        af(sgn[:, d, h, :], bank[:, :], ACT.Sigmoid, scale=-1.0).then_inc(A_free, 1)
                elif kind == "q":
                    for c in range(2):
                        bank = turn_in(*pieces[c])
                        af(qT[:, 2 * step[1] + c, :], bank[:, :], ACT.Silu).then_inc(A_free, 1)
                elif kind == "v":
                    for t in range(NT):
                        bank = turn_in(*pieces[t])
                        af(v[:, t, step[1] * WCOLS:(step[1] + 1) * WCOLS], bank[:, 0:WCOLS], ACT.Copy).then_inc(A_free, 1)
                elif kind == "logf":
                    act.wait_ge(lb_done, 1)
                    act.wait_ge(A_free, n_of("A", ("z", 1, 1, 1)))
                    for h in range(H):
                        for d in range(2):
                            u = 4 * d + h
                            af(sig[:, d, h, :], sig[:, d, h, :], ACT.Ln, scale=lbs[:, 1, u:u + 1],
                               bias=lbs[:, 0, u:u + 1]).then_inc(logf_done, 1)
                elif kind == "elem":
                    _, h, d = step
                    u = 2 * h + d
                    act.wait_ge(dsub, 2 * u + 2)
                    af(expn[d][:, :], dref[d][:, :], ACT.Exp, scale=-1.0).then_inc(exps, 1)
                    af(dlast[d][:, :], dlast[d][:, :], ACT.Exp).then_inc(exps, 1)
                    af(cumG[d][:, :], cumG[d][:, :], ACT.Exp).then_inc(exps, 1)
                    act.wait_ge(exps, 4 * u + 1)
                    af(dref[d][:, :], dref[d][:, :], ACT.Exp).then_inc(exps, 1)
                elif kind == "intra":
                    _, h, d = step
                    u = 2 * h + d
                    act.wait_ge(kd_turned, u + 1)
                    act.wait_ge(zero_done, 2)
                    for i in range(2):
                        rows = slice(CH * i, CH * i + CH)
                        last = af(kdn[d][rows, :, i, :], tp[rows, :].rearrange("p (j e) -> p j e", j=NT), ACT.Copy)
                    last.then_inc(kd_copied, 1)
                elif kind == "o":
                    h = step[1]
                    act.wait_ge(o_made, h + 1)
                    af(oT[:, h, :], tp[:, :], ACT.Copy).then_inc(o_kept, 1)
                elif kind == "conv" and step[4] == "C":
                    _, f, b, c, _ = step
                    n = window(f)[1]
                    bank = turn_in(*pieces[0])
                    g = (f * 2 + b) * 2 + c
                    if f:
                        act.wait_ge(y0_done, H * f)
                    if g >= 2:
                        act.wait_ge(y1_done, g - 1)
                    af(csb[:, c, 0:n], bank[:, 0:n], ACT.Copy).then_inc(A_free, 1)
                elif kind == "mq":
                    _, f, b, c = step
                    bank = turn_in(*pieces[0])
                    if f:
                        act.wait_ge(top1_done, QH * TPH * f)
                    af(mqT[:, 2 * b + c, :], bank[:, 0:HALF], ACT.Copy).then_inc(A_free, 1)
                elif kind == "logits":
                    _, f, h = step
                    u = H * f + h
                    act.wait_ge(o_kept, H)
                    act.wait_ge(B_free, n_of("B", last_before_hg[f]))
                    if h >= 2:
                        act.wait_ge(A_full, n_of("A", ("hg", f, (h - 2) // 2, h % 2, "ss")))
                    af(tmp[:, h % 2, :], oT[:, h, f * HALF:(f + 1) * HALF], ACT.Square).then_inc(osq_done, 1)
                    act.wait_ge(mx_done, u + 1)
                    if u >= 1:
                        act.wait_ge(p_turned, u)
                    for t in range(TPH):
                        af(prob[:, t, :], scb[:, t * NMEM:(t + 1) * NMEM], ACT.Exp, scale=float(P) ** -0.5,
                           bias=tiny[:, t:t + 1], accum_out=tiny[:, 4 + t:5 + t]).then_inc(pexp, 1)
                elif kind == "turn_p":
                    _, f, h = step
                    u = H * f + h
                    act.wait_ge(p_turned, u + 1)
                    if u >= 1:
                        act.wait_ge(pv_made, u)
                    af(probT, tp[:, :].rearrange("p (m t) -> p m t", m=2), ACT.Copy).then_inc(pT_done, 1)
                elif kind == "values":
                    _, f, h = step
                    u = H * f + h
                    act.wait_ge(pv_made, u + 1)
                    af(y[2][:, h, :], tp[:, 0:HALF], ACT.Copy).then_inc(y2_done, 1)
                elif kind == "branch":
                    _, f, n, b, c = step
                    bank = turn_in(*pieces[0])
                    before = [k for k in order["B"][:place["B"][pieces[1][1]]] if k[0] == "branch"][-2:]
                    if len(before) == 2:
                        act.wait_ge(B_free, n_of("B", before[0]))
                    if ("hg_mul", f, H - 1) in steps[:steps.index(step)]:
                        act.wait_ge(y0_done, H * (f + 1))
                    af(gsb[:, c, :], bank[:, 0:HALF], ACT.Sigmoid).then_inc(A_free, 1)
                elif kind == "hg":
                    _, f, b, c = step
                    h = 2 * b + c
                    if f * H + h >= 2:
                        act.wait_ge(y0_done, f * H + h - 1)
                    bank = turn_in(*pieces[0])
                    af(csb[:, c, 0:HALF], bank[:, 0:HALF], ACT.Silu).then_inc(A_free, 1)
                    bank = turn_in(*pieces[1])
                    af(gsb[:, c, :], bank[:, 0:HALF], ACT.Sqrt, scale=1.0 / P, bias=eps[:, :]).then_inc(A_free, 1)
                elif kind == "ffn":
                    f = step[1]
                    for t in range(TPH):
                        act.wait_ge(B_free, n_of("B", ("wout", f, 3, TPH - 1)))
                        then_wait(af(junk[:, :], x2[:, t, :], ACT.Square, accum_out=tiny[:, 8 + t:9 + t]))
                        af(tiny[:, 10 + t:11 + t], tiny[:, 8 + t:9 + t], ACT.Sqrt, scale=1.0 / D,
                           bias=eps[:, :]).then_inc(ssq_done, 1)
                elif kind == "turn":
                    _, f, t = step
                    for g, (r, key) in enumerate(pieces):
                        bank = turn_in(r, key)
                        af(merged[:, 4 * g:4 * g + 4, t * P:t * P + P], bank[:, :].rearrange("p (k t) -> p k t", k=4),
                           ACT.Copy).then_inc(A_free, 1)
                elif kind == "query":
                    _, f, b, c = step
                    bank = turn_in(*pieces[0])
                    if b or f:
                        act.wait_ge(A_full, n_of("A", ("keys", f, b - 1, c) if b else ("keys", f - 1, HP // 2 - 1, c)))
                    af(qpT[:, c, :], bank[:, 0:HALF], ACT.Copy).then_inc(A_free, 1)
                elif kind == "keys":
                    _, f, b = step
                    for c, (r, key) in enumerate(pieces):
                        hp = 2 * b + c
                        bank = turn_in(r, key)
                        af(score[:, :, hp * NK:hp * NK + NK], bank[:, 0:TPH * P].rearrange("p (t k) -> p t k", t=TPH),
                           ACT.Copy).then_inc(A_free, 1)
                elif kind == "look":
                    _, t, g = step
                    bq = bs[:, HQ * g:HQ * (g + 1), :]
                    act.wait_ge(gd_done, QH * t + g + 1)
                    af(bq, bq, ACT.Exp).then_inc(ge_done, 1)
                elif kind == "gather":
                    _, t, k, n = step
                    act.wait_ge(gate_done, QH * t + (k + n - 1) // (SLOTS // QH) + 1)
                    whole = n // RING
                    if whole > 1:
                        with act.Fori(0, whole) as it:
                            gather_body(t, k, RING, it)
                    else:
                        whole = 0
                    if n > whole * RING:
                        gather_body(t, k + whole * RING, n - whole * RING, 0)
                elif kind == "last":
                    t = step[1]
                    act.wait_ge(drained, t + 1)
                    then_wait(af(junk[:, :], h2[:, t, :], ACT.Square, accum_out=tiny[:, 16:17]))
                    af(tiny[:, 17:18], tiny[:, 16:17], ACT.Sqrt, scale=1.0 / D, bias=eps[:, :]).then_inc(fsq, 1)
                elif kind == "store":
                    t = step[1]
                    act.wait_ge(fdone, t + 1)
                    act.dma_start(outn[t], h2[:, t, :]).then_inc(out_done, 16)
            act.wait_ge(out_done, 16 * NT)

        @block.vector
        def _(dve):
            done = [0]
            ve = nc.vector

            def tick(ins):
                done[0] += 1
                ins.then_inc(v_ord, 1)

            def settle():
                dve.wait_ge(v_ord, done[0])

            def link(ins):
                tick(ins)
                settle()

            def turn_in(r, key):
                dve.wait_ge(full[r], n_of(r, key))
                return bank_of(r, key)

            def dots(t, k, n, it):
                for i in range(n):
                    g = t * SLOTS + k + i
                    s = g % RING
                    dve.wait_ge(landed[s], it * 16 + land_count(g))
                    ve.tensor_tensor_reduce(ring[:, s, 0:D], ring[:, s, 0:D], h2[:, t, :], 1.0, 0.0, ALU.mult, ALU.add,
                                            acts[:, 0, s:s + 1]).then_inc(dot, 1)

            for step in steps:
                kind = step[0]
                pieces = chunks_of(step)
                if kind == "norm_mem":
                    dve.wait_ge(c_in, 32)
                    l0, l1 = vec[:, V_LB:V_LB + 8], vec[:, V_LB + 8:V_LB + 16]
                    ve.memset(eps[:, :], EPS).then_inc(eps_done, 1)
                    link(ve.tensor_tensor(lbs[:, 2, :], l0, l1, ALU.max))
                    ve.tensor_tensor(lbs[:, 0, :], l0, lbs[:, 2, :], ALU.subtract).then_inc(lb_diff, 1)
                    ve.tensor_tensor(lbs[:, 1, :], l1, lbs[:, 2, :], ALU.subtract).then_inc(lb_diff, 1)
                if kind in ("norm_in", "norm_mem"):
                    src_t, n, g0, dn = (hT, T, V_MIX, h_done) if kind == "norm_in" else (memT, NMEM, V_MEM, m_done)
                    r, key = pieces[0]
                    bank = turn_in(r, key)
                    dve.wait_ge(root, 1 + (kind == "norm_in"))
                    link(ve.reciprocal(bank[:, 0:n], bank[:, 0:n]))
                    for k in range(KD):
                        last = ve.scalar_tensor_tensor(out=src_t[:, k, :], in0=src_t[:, k, :], scalar=vec[:, g0 + k:g0 + k + 1],
                                                       in1=bank[:, 0:n], op0=ALU.mult, op1=ALU.mult)
                        last.then_inc(dn, 1)
                    if r == "B":
                        dve.wait_ge(h_done, KD)
                        dve.sem_inc(B_free, 1)
                elif step == ("z", 0, 0):
                    dve.wait_ge(hc_in, 16)
                    dve.wait_ge(lb_exp, 1)
                    link(ve.tensor_tensor(lbs[:, 2, :], lbs[:, 0, :], lbs[:, 1, :], ALU.add))
                    link(ve.reciprocal(lbs[:, 2, :], lbs[:, 2, :]))
                    link(ve.tensor_tensor(lbs[:, 0, :], lbs[:, 0, :], lbs[:, 2, :], ALU.mult))
                    ve.tensor_scalar(lbs[:, 1, :], lbs[:, 0, :], -1.0, 1.0, ALU.mult, ALU.add).then_inc(lb_done, 1)
                    for d in range(2):
                        tick(ve.memset(PT[d][:, :], 0.0))
                    for d in range(2):
                        ve.memset(kdn[d][:, :, :, :], 0.0).then_inc(zero_done, 1)
                    ve.memset(ub[:, :, :], 0.0).then_inc(zero_done, 1)
                elif kind == "elem":
                    _, h, d = step
                    u = 2 * h + d
                    dve.wait_ge(logf_done, u + 1)
                    dve.wait_ge(A_free, n_of("A", ("q", 1, 1)))
                    if h >= 1:
                        dve.wait_ge(o_made, h)
                    lf = sig[:, d, h, :]
                    G = cumG[d]
                    if d == 0:
                        link(ve.tensor_tensor_scan(G[:, :], hcst[:, S_KEEP:S_KEEP + T], lf, 0.0, ALU.mult, ALU.add))
                    else:
                        link(ve.tensor_tensor_scan(G[:, ::-1], hcst[:, S_KEEP:S_KEEP + T], lf[:, ::-1], 0.0, ALU.mult, ALU.add))
                    mid, end = (CH // 2 - 1, CH - 1) if d == 0 else (CH // 2, 0)
                    Gc = G[:, :].rearrange("p (n c) -> p n c", c=CH)
                    ve.tensor_tensor(dref[d][:, :].rearrange("p (n c) -> p n c", c=CH), Gc,
                                     Gc[:, :, mid:mid + 1].to_broadcast([P, NCH, CH]), ALU.subtract).then_inc(dsub, 1)
                    ve.tensor_tensor(dlast[d][:, :].rearrange("p (n c) -> p n c", c=CH),
                                     Gc[:, :, end:end + 1].to_broadcast([P, NCH, CH]), Gc, ALU.subtract).then_inc(dsub, 1)
                    lb1 = lbs[:, 1, 4 * d + h:4 * d + h + 1]
                    k_ = sgn[:, d, h, :]
                    dve.wait_ge(exps, 4 * u + 1)
                    ve.scalar_tensor_tensor(out=expn[d][:, :], in0=k_, scalar=lb1, in1=expn[d][:, :],
                                            op0=ALU.mult, op1=ALU.mult).then_inc(prods, 1)
                    dve.wait_ge(exps, 4 * u + 2)
                    ve.scalar_tensor_tensor(out=dlast[d][:, :], in0=k_, scalar=lb1, in1=dlast[d][:, :],
                                            op0=ALU.mult, op1=ALU.mult).then_inc(prods, 1)
                    dve.wait_ge(exps, 4 * u + 4)
                    tick(ve.tensor_copy(decay[d][:, :], Gc[:, :, end]))
                    ve.tensor_tensor(dref[d][:, :], dref[d][:, :], qT[:, h, :], ALU.mult).then_inc(prods, 1)
                    settle()
                    ve.tensor_tensor(G[:, :], G[:, :], qT[:, h, :], ALU.mult).then_inc(prods, 1)
                elif kind == "intra":
                    _, h, d = step
                    u = 2 * h + d
                    dve.wait_ge(sc_made, u + 1)
                    settle()
                    m = hcst[:, (S_MF, S_MB)[d]:(S_MF, S_MB)[d] + P].bitcast(U32)
                    ve.copy_predicated(PT[d][:, :].rearrange("p (j t) -> p j t", j=NT),
                                       m.unsqueeze(1).to_broadcast([P, NT, P]),
                                       scb[:, :].rearrange("p (j t) -> p j t", j=NT)).then_inc(sc_masked, 1)
                    dve.wait_ge(ds_made, u + 1)
                    seq = list(range(NCH)) if d == 0 else list(range(NCH - 1, -1, -1))
                    st = state[d]
                    for i in range(NCH - 1):
                        n, nx = seq[i], seq[i + 1]
                        dS = wide[:, n * P:n * P + P]
                        if i == 0:
                            ins = ve.tensor_copy(st[:, nx, :], dS)
                        else:
                            ins = ve.scalar_tensor_tensor(out=st[:, nx, :], in0=st[:, n, :], scalar=decay[d][:, n:n + 1],
                                                          in1=dS, op0=ALU.mult, op1=ALU.add)
                        if i < NCH - 2:
                            link(ins)
                        else:
                            ins.then_inc(st_done, 1)
                elif kind == "conv" and step[4] == "h":
                    _, f, b, c, _ = step
                    t0, n, c0 = window(f)
                    ch = 2 * b + c
                    bank = turn_in(*pieces[0])
                    dve.wait_ge(A_free, n_of("A", (*step[:4], "C")))
                    dve.wait_ge(zero_done, 3)
                    if f == 1 and b == 0:
                        link(ve.memset(ub[:, c, HALF + 1:HALF + 2], 0.0))
                    ve.tensor_tensor(ub[:, c, c0:c0 + n], csb[:, c, 0:n], bank[:, 0:n], ALU.mult).then_inc(B_free, 1)
                    dve.wait_ge(B_free, n_of(*pieces[0]))
                    w = [vec[:, V_CONV + 4 * j + ch:V_CONV + 4 * j + ch + 1] for j in range(3)]
                    yc = y[1][:, ch, :]
                    if f == 1 and ch == 0:
                        settle()
                    link(ve.tensor_scalar(yc, ub[:, c, 0:HALF], w[0], None, ALU.mult))
                    for j in (1, 2):
                        link(ve.scalar_tensor_tensor(out=yc, in0=ub[:, c, j:j + HALF], scalar=w[j], in1=yc,
                                                     op0=ALU.mult, op1=ALU.add))
                elif kind == "conv" and step[4] == "B":
                    yc = y[1][:, 2 * step[2] + step[3], :]
                    bank = turn_in(*pieces[0])
                    link(ve.tensor_tensor(yc, yc, bank[:, 0:HALF], ALU.mult))
                    dve.sem_inc(B_free, 1)
                    dve.sem_inc(y1_done, 1)
                elif kind == "logits":
                    _, f, h = step
                    u = H * f + h
                    dve.wait_ge(lg_made, u + 1)
                    link(ve.tensor_reduce(tiny[:, 2:4], scb[:, :].rearrange("p (t m) -> p t m", t=TPH), AX_X, ALU.max))
                    if u:
                        dve.wait_ge(pexp, TPH * u)
                    ve.tensor_scalar(tiny[:, 0:2], tiny[:, 2:4], -float(P) ** -0.5, None, ALU.mult).then_inc(mx_done, 1)
                elif kind == "norm_att":
                    u = H * step[1] + step[2]
                    dve.wait_ge(pexp, TPH * (u + 1))
                    link(ve.reciprocal(tiny[:, 6:8], tiny[:, 4:6]))
                    for t in range(TPH):
                        ins = ve.tensor_scalar(prob[:, t, :], prob[:, t, :], tiny[:, 6 + t:7 + t], None, ALU.mult)
                        tick(ins) if t == 0 else ins.then_inc(pnorm, 1)
                elif kind == "branch":
                    _, f, n, b, c = step
                    dc = 2 * b + c
                    dve.wait_ge(A_free, n_of(*pieces[0]))
                    bank = turn_in(*pieces[1])
                    if n == BRANCH_ORDER[0]:
                        ve.tensor_tensor(merged[:, dc, :], gsb[:, c, :], bank[:, 0:HALF], ALU.mult).then_inc(B_free, 1)
                    else:
                        link(ve.tensor_tensor(gsb[:, c, :], gsb[:, c, :], bank[:, 0:HALF], ALU.mult))
                        ve.tensor_tensor(merged[:, dc, :], merged[:, dc, :], gsb[:, c, :], ALU.add).then_inc(B_free, 1)
                elif kind == "hg_mul":
                    _, f, h = step
                    c = h % 2
                    dve.wait_ge(A_free, n_of("A", ("hg", f, h // 2, c, "ss")))
                    link(ve.reciprocal(gsb[:, c, :], gsb[:, c, :]))
                    link(ve.scalar_tensor_tensor(out=gsb[:, c, :], in0=oT[:, h, f * HALF:(f + 1) * HALF],
                                                 scalar=vec[:, V_HG + h:V_HG + h + 1], in1=gsb[:, c, :],
                                                 op0=ALU.mult, op1=ALU.mult))
                    ve.tensor_tensor(y[0][:, h, :], gsb[:, c, :], csb[:, c, 0:HALF], ALU.mult).then_inc(y0_done, 1)
                elif kind == "wout":
                    _, f, b, t = step
                    bank = turn_in(*pieces[0])
                    dve.wait_ge(x_nat, 16 * TPH * (f + 1))
                    cols = slice(b * WCOLS, (b + 1) * WCOLS)
                    ve.tensor_tensor(x2[:, t, cols], x2[:, t, cols], bank[:, 0:WCOLS], ALU.add).then_inc(B_free, 1)
                elif kind == "ffn":
                    f = step[1]
                    dve.wait_ge(late_in, 48)
                    for t in range(TPH):
                        dve.wait_ge(ssq_done, TPH * f + t + 1)
                        link(ve.reciprocal(tiny[:, 12 + t:13 + t], tiny[:, 10 + t:11 + t]))
                        ve.scalar_tensor_tensor(out=h2[:, TPH * f + t, :], in0=x2[:, t, :], scalar=tiny[:, 12 + t:13 + t],
                                                in1=g_ffn[:, :], op0=ALU.mult, op1=ALU.mult).then_inc(h2_done, 1)
                elif kind == "best":
                    _, t, g = step
                    f, tl = t // TPH, t % TPH
                    dve.wait_ge(A_free, n_of("A", ("keys", f, HQ * (g + 1) - 1, 1)))
                    hps = range(2 * HQ * g, 2 * HQ * (g + 1))
                    hs = range(HQ * g, HQ * (g + 1))
                    sc = lambda hp: score[:, tl, hp * NK:hp * NK + NK]

                    def best16(items, value, where, source):
                        for o_ in (0, 8):
                            settle()
                            for i in items:
                                tick(ve.max(value[:, i, o_:o_ + 8], source(i)))
                            settle()
                            for i in items:
                                tick(ve.max_index(where[:, i, o_:o_ + 8], value[:, i, o_:o_ + 8], source(i)))
                            if o_ == 0:
                                settle()
                                for i in items:
                                    tick(ve.match_replace(source(i), value[:, i, 0:8], source(i), NEG))

                    best16(hps, tv, ti, sc)
                    settle()
                    a0, a1 = hps[0], hps[-1] + 1
                    h0, h1 = hs[0], hs[-1] + 1
                    dve.sem_inc(top1_done, 1)
                    link(ve.tensor_copy(tif[:, a0:a1, :], ti[:, a0:a1, :]))
                    tif4 = tif[:, a0:a1, :].rearrange("p (h s) k -> p h s k", s=2)
                    tv4 = tv[:, a0:a1, :].rearrange("p (h s) k -> p h s k", s=2)
                    link(ve.tensor_scalar(tif4[:, :, 0, :], tif4[:, :, 0, :], float(NK), None, ALU.mult))
                    for dst, s4 in ((cs, tv4), (ci, tif4)):
                        off = 0
                        for i0, ni, nj in CAND_ROWS:
                            o_ = dst[:, h0:h1, off:off + ni * nj].rearrange("p h (i j) -> p h i j", i=ni)
                            tick(ve.tensor_tensor(o_, s4[:, :, 0, i0:i0 + ni].unsqueeze(3).to_broadcast([P, HQ, ni, nj]),
                                                  s4[:, :, 1, 0:nj].unsqueeze(2).to_broadcast([P, HQ, ni, nj]), ALU.add))
                            off += ni * nj
                    if QH * t + g:
                        dve.wait_ge(gate_done, QH * t + g)
                    best16(hs, bs, pos, lambda h: cs[:, h, :])
                elif kind == "look":
                    _, t, g = step
                    h0, h1 = HQ * g, HQ * (g + 1)
                    bq, pq_ = bs[:, h0:h1, :], posf[:, h0:h1, :]
                    settle()
                    if QH * t + g:
                        dve.wait_ge(idx_done, QH * t + g)
                    tick(ve.tensor_copy(pq_, pos[:, h0:h1, :]))
                    link(ve.tensor_copy(tiny[:, 24 + h0:24 + h1], bs[:, h0:h1, 0]))
                    ve.tensor_tensor(bq, bq, tiny[:, 24 + h0:24 + h1].unsqueeze(2).to_broadcast([P, HQ, TOP]),
                                     ALU.subtract).then_inc(gd_done, 1)
                    iota = cst[:, C_IOTA:C_IOTA + NCAND].unsqueeze(1).to_broadcast([P, TOP, NCAND])
                    for h in range(h0, h1):
                        link(ve.tensor_tensor(eq[:, :, :], iota, posf[:, h, :].unsqueeze(2).to_broadcast([P, TOP, NCAND]),
                                              ALU.is_equal))
                        link(ve.tensor_tensor(eq[:, :, :], eq[:, :, :], ci[:, h, :].unsqueeze(1).to_broadcast([P, TOP, NCAND]),
                                              ALU.mult))
                        link(ve.tensor_reduce(posf[:, h, :], eq[:, :, :], AX_X, ALU.add))
                    ve.tensor_copy(idx[:, t, h0 * TOP:h1 * TOP], pq_.rearrange("p h k -> p (h k)")).then_inc(idx_done, 1)
                    dve.wait_ge(ge_done, QH * t + g + 1)
                    link(ve.tensor_reduce(tiny[:, 24 + h0:24 + h1], bq, AX_X, ALU.add))
                    link(ve.reciprocal(tiny[:, 24 + h0:24 + h1], tiny[:, 24 + h0:24 + h1]))
                    ve.tensor_tensor(gate[:, t, h0 * TOP:h1 * TOP].rearrange("p (h k) -> p h k", h=HQ), bq,
                                     tiny[:, 24 + h0:24 + h1].unsqueeze(2).to_broadcast([P, HQ, TOP]),
                                     ALU.mult).then_inc(gate_done, 1)
                elif kind == "gather":
                    _, t, k, n = step
                    whole = n // RING
                    if whole > 1:
                        with dve.Fori(0, whole) as it:
                            dots(t, k, RING, it)
                    else:
                        whole = 0
                    dots(t, k + whole * RING, n - whole * RING, 0)
                elif kind == "drain":
                    t = step[1]
                    dve.wait_ge(used, RING + (t + 1) * SLOTS)
                    dve.wait_ge(dot, (t + 1) * SLOTS)
                    ve.tensor_copy(h2[:, t, :], wide[:, :]).then_inc(drained, 1)
                elif kind == "last":
                    t = step[1]
                    dve.wait_ge(fsq, t + 1)
                    link(ve.reciprocal(tiny[:, 18:19], tiny[:, 17:18]))
                    ve.scalar_tensor_tensor(out=h2[:, t, :], in0=h2[:, t, :], scalar=tiny[:, 18:19], in1=g_fin[:, :],
                                            op0=ALU.mult, op1=ALU.mult).then_inc(fdone, 1)


def kernel(**inp):
    import numpy as _np
    import concourse.bacc as _bacc
    from concourse.bass_utils import run_bass_kernel_spmd as _run

    def cols(v_):
        return _np.asarray(v_).reshape(-1, P).T

    g = {k: _np.asarray(v_) for k, v_ in inp.items()}
    vec = _np.concatenate([cols(g["norm_mix_g"][0]), cols(g["mem_norm_g"][0]), cols(g["hg_lb"][0].reshape(-1)),
                           cols(g["hg_lb"][1].reshape(-1)), cols(g["hg_norm_g"][0]), cols(g["sc_conv_w"][0].reshape(-1))], axis=1)
    arrays = {
        "xT": g["x"][0].T, "x": g["x"][0], "memT": g["mem"][0].T, "cst": constants()[0], "hcst": constants()[1], "vec": vec,
        "w_in": g["w_in"][0], "w_kv": g["w_mem_kv"][0], "w_br": g["w_branch"][0].reshape(3 * BW, D),
        "w_out": g["w_out"][0], "w_pq": g["peer_w_q"][0],
        "keys": g["peer_sub_keys"][0].reshape(HP, NK, P).transpose(2, 0, 1).reshape(P, HP * NK),
        "g_ffn": _np.broadcast_to(g["norm_ffn_g"][0], (P, D)), "g_fin": _np.broadcast_to(g["final_norm_g"], (P, D)),
        "uv": _np.concatenate([g["peer_u"][0], g["peer_v"][0]], axis=1),
    }
    arrays = {k: _np.ascontiguousarray(v_) for k, v_ in arrays.items()}
    nc = _bacc.Bacc("TRN2", target_bir_lowering=False, num_devices=1)
    args = {k: nc.dram_tensor(f"in_{k}", v_.shape, F32, kind="ExternalInput").ap() for k, v_ in arrays.items()}
    out = nc.dram_tensor("out_y", (1, T, D), F32, kind="ExternalOutput").ap()
    build(nc, args, out)
    r = _run(nc, [{f"in_{k}": v_ for k, v_ in arrays.items()}], core_ids=[0])
    return r.results[0]["out_y"]
```
